# Optimizing a Trainium2 kernel written in Bass

```python
import math
import jax, jax.numpy as jnp
from jax import lax
import numpy as np

D_MODEL = 1024
BATCH = 1
SEQ = 256
DEPTH = 1

D_CONV = D_MODEL
CONV_WIDTH = 31
N_HEADS = 8
HEAD_DIM = 64
V_DIM = 2 * HEAD_DIM
ROT_DIM = HEAD_DIM // 4
ROPE_THETA = 500000.0
Q_BLOCK = 128
QK_W = N_HEADS * 2 * HEAD_DIM
V_W = N_HEADS * V_DIM
N_EXPERTS = 32
TOP_K = 4
D_FF = D_MODEL
SWIGLU_ALPHA = 1.702
SWIGLU_LIMIT = 7.0
EPS = 1e-6
IN_COLS = 2 * D_CONV + 2 * QK_W + V_W + 2 * D_MODEL

kernel_name = 'hybrid_conformer_diffattn_moe_block'

def rms_norm(x, g):
    xf = x.astype(jnp.float32)
    y = xf * lax.rsqrt(jnp.mean(xf * xf, axis=-1, keepdims=True) + EPS)
    return (y * g.astype(jnp.float32)).astype(x.dtype)

def layer_norm(x, g, b):
    xf = x.astype(jnp.float32)
    mu = jnp.mean(xf, axis=-1, keepdims=True)
    var = jnp.mean(jnp.square(xf - mu), axis=-1, keepdims=True)
    y = (xf - mu) * lax.rsqrt(var + EPS)
    return (y * g.astype(jnp.float32) + b.astype(jnp.float32)).astype(x.dtype)

def rope_tables(positions):
    inv = ROPE_THETA ** (-jnp.arange(0, ROT_DIM, 2, dtype=jnp.float32) / ROT_DIM)
    ang = positions.astype(jnp.float32)[..., None] * inv
    return jnp.cos(ang)[:, :, None, None, :], jnp.sin(ang)[:, :, None, None, :]

def partial_rope(t, cos, sin):
    rot, rest = t[..., :ROT_DIM], t[..., ROT_DIM:]
    x1, x2 = rot[..., :ROT_DIM // 2], rot[..., ROT_DIM // 2:]
    rot = jnp.concatenate([x1 * cos - x2 * sin, x2 * cos + x1 * sin], axis=-1)
    return jnp.concatenate([rot.astype(t.dtype), rest], axis=-1)

def conformer_conv(u_glu, conv_w, conv_b, ln_g, ln_b, w_out, b_out):
    a, gt = jnp.split(u_glu, 2, axis=-1)
    u = a * jax.nn.sigmoid(gt)
    u = lax.conv_general_dilated(
        u, conv_w[:, None, :], window_strides=(1,),
        padding=[(CONV_WIDTH - 1, 0)],
        dimension_numbers=('NWC', 'WIO', 'NWC'),
        feature_group_count=D_CONV) + conv_b
    u = jax.nn.silu(layer_norm(u, ln_g, ln_b))
    return u @ w_out + b_out

def diff_attention(q, k, v, lam, lam_init, subln_g):
    B, S = q.shape[0], q.shape[1]
    nb = S // Q_BLOCK
    scale = HEAD_DIM ** -0.5
    qb = q.reshape(B, nb, Q_BLOCK, N_HEADS, 2, HEAD_DIM).transpose(1, 0, 2, 3, 4, 5)
    k_pos = jnp.arange(S)

    def block(args):
        qi, i = args
        s = jnp.einsum('bqhcd,bkhcd->bhcqk', qi, k,
                       preferred_element_type=jnp.float32) * scale
        q_pos = i * Q_BLOCK + jnp.arange(Q_BLOCK)
        causal = k_pos[None, :] <= q_pos[:, None]
        p = jax.nn.softmax(jnp.where(causal, s, -jnp.inf), axis=-1)
        a = p[:, :, 0] - lam * p[:, :, 1]
        return jnp.einsum('bhqk,bkhe->bqhe', a.astype(v.dtype), v)

    o = lax.map(block, (qb, jnp.arange(nb)))
    o = o.transpose(1, 0, 2, 3, 4).reshape(B, S, N_HEADS, V_DIM)
    o = rms_norm(o, subln_g) * (1.0 - lam_init)
    return o.reshape(B, S, V_W)

def mixer(h, cos, sin, w_in, conv_w, conv_b, conv_ln_g, conv_ln_b, w_conv_out, b_conv_out,
          q_norm_g, k_norm_g, lambda_q1, lambda_k1, lambda_q2, lambda_k2, lam_init,
          subln_g, w_attn_out, b_gate, w_o):
    B, S = h.shape[0], h.shape[1]
    u = h @ w_in
    c0 = 2 * D_CONV
    u_conv, q, k, v, g = jnp.split(
        u, [c0, c0 + QK_W, c0 + 2 * QK_W, c0 + 2 * QK_W + V_W], axis=-1)
    y_conv = conformer_conv(u_conv, conv_w, conv_b, conv_ln_g, conv_ln_b, w_conv_out, b_conv_out)
    q = partial_rope(rms_norm(q.reshape(B, S, N_HEADS, 2, HEAD_DIM), q_norm_g), cos, sin)
    k = partial_rope(rms_norm(k.reshape(B, S, N_HEADS, 2, HEAD_DIM), k_norm_g), cos, sin)
    v = v.reshape(B, S, N_HEADS, V_DIM)
    lam = (jnp.exp(jnp.sum(lambda_q1 * lambda_k1).astype(jnp.float32))
           - jnp.exp(jnp.sum(lambda_q2 * lambda_k2).astype(jnp.float32)) + lam_init)
    y_attn = diff_attention(q, k, v, lam, lam_init, subln_g) @ w_attn_out
    g_conv, g_attn = jnp.split(jax.nn.sigmoid(g + b_gate), 2, axis=-1)
    return (g_conv * y_conv + g_attn * y_attn) @ w_o

def moe(h, w_router, b_router, w_up, b_up, w_down, b_down):
    B, S, D = h.shape
    t = h.reshape(B * S, D)
    logits = (t @ w_router + b_router).astype(jnp.float32)
    top_vals, top_idx = lax.top_k(logits, TOP_K)
    wts = jax.nn.softmax(top_vals, axis=-1)
    combine = jnp.sum(jax.nn.one_hot(top_idx, N_EXPERTS, dtype=jnp.float32) * wts[..., None],
                      axis=1).astype(t.dtype)
    y = jnp.zeros_like(t)
    for e in range(N_EXPERTS):
        gu = t @ w_up[e] + b_up[e]
        glu = jnp.minimum(gu[:, 0::2], SWIGLU_LIMIT)
        lin = jnp.clip(gu[:, 1::2], -SWIGLU_LIMIT, SWIGLU_LIMIT)
        act = glu * jax.nn.sigmoid(SWIGLU_ALPHA * glu) * (lin + 1.0)
        y = y + combine[:, e:e + 1] * (act @ w_down[e] + b_down[e])
    return y.reshape(B, S, D)

def setup_inputs(seed: int = 0) -> dict:
    key = jax.random.key(seed)
    ks = jax.random.split(key, 32)
    f32 = jnp.float32
    L = DEPTH

    def nrm(k, shape, scale):
        return jax.random.normal(k, shape, f32) * scale

    return {
        'x': nrm(ks[0], (BATCH, SEQ, D_MODEL), 1.0),
        'c': nrm(ks[1], (BATCH, D_MODEL), 1.0),
        'positions': (jnp.arange(SEQ, dtype=jnp.int32)[None, :]
                      + jax.random.randint(ks[2], (BATCH, 1), 0, 1024, dtype=jnp.int32)),
        'w_ada': nrm(ks[3], (L, D_MODEL, 6 * D_MODEL), 0.5 * D_MODEL ** -0.5),
        'b_ada': nrm(ks[4], (L, 6 * D_MODEL), 0.02),
        'norm1_g': 1.0 + nrm(ks[5], (L, D_MODEL), 0.1),
        'w_in': nrm(ks[6], (L, D_MODEL, IN_COLS), D_MODEL ** -0.5),
        'conv_w': nrm(ks[7], (L, CONV_WIDTH, D_CONV), CONV_WIDTH ** -0.5),
        'conv_b': nrm(ks[8], (L, D_CONV), 0.02),
        'conv_ln_g': 1.0 + nrm(ks[9], (L, D_CONV), 0.1),
        'conv_ln_b': nrm(ks[10], (L, D_CONV), 0.02),
        'w_conv_out': nrm(ks[11], (L, D_CONV, D_MODEL), D_CONV ** -0.5),
        'b_conv_out': nrm(ks[12], (L, D_MODEL), 0.02),
        'q_norm_g': 1.0 + nrm(ks[13], (L, HEAD_DIM), 0.1),
        'k_norm_g': 1.0 + nrm(ks[14], (L, HEAD_DIM), 0.1),
        'lambda_q1': nrm(ks[15], (L, HEAD_DIM), 0.1),
        'lambda_k1': nrm(ks[16], (L, HEAD_DIM), 0.1),
        'lambda_q2': nrm(ks[17], (L, HEAD_DIM), 0.1),
        'lambda_k2': nrm(ks[18], (L, HEAD_DIM), 0.1),
        'subln_g': 1.0 + nrm(ks[19], (L, V_DIM), 0.1),
        'w_attn_out': nrm(ks[20], (L, V_W, D_MODEL), V_W ** -0.5),
        'b_gate': nrm(ks[21], (L, 2 * D_MODEL), 0.02),
        'w_o': nrm(ks[22], (L, D_MODEL, D_MODEL), D_MODEL ** -0.5),
        'norm2_g': 1.0 + nrm(ks[23], (L, D_MODEL), 0.1),
        'w_router': nrm(ks[24], (L, D_MODEL, N_EXPERTS), D_MODEL ** -0.5),
        'b_router': nrm(ks[25], (L, N_EXPERTS), 0.01),
        'w_up': nrm(ks[26], (L, N_EXPERTS, D_MODEL, 2 * D_FF), D_MODEL ** -0.5),
        'b_up': nrm(ks[27], (L, N_EXPERTS, 2 * D_FF), 0.02),
        'w_down': nrm(ks[28], (L, N_EXPERTS, D_FF, D_MODEL), D_FF ** -0.5),
        'b_down': nrm(ks[29], (L, N_EXPERTS, D_MODEL), 0.02),
    }

def reference(x, c, positions, w_ada, b_ada, norm1_g, w_in, conv_w, conv_b, conv_ln_g, conv_ln_b,
              w_conv_out, b_conv_out, q_norm_g, k_norm_g, lambda_q1, lambda_k1, lambda_q2, lambda_k2,
              subln_g, w_attn_out, b_gate, w_o, norm2_g, w_router, b_router, w_up, b_up, w_down, b_down):
    cos, sin = rope_tables(positions)
    c_act = jax.nn.silu(c)
    for l in range(DEPTH):
        lam_init = 0.8 - 0.6 * math.exp(-0.3 * l)
        mod = (c_act @ w_ada[l] + b_ada[l])[:, None, :]
        shift1, scale1, gate1, shift2, scale2, gate2 = jnp.split(mod, 6, axis=-1)
        h = rms_norm(x, norm1_g[l]) * (1.0 + scale1) + shift1
        x = x + gate1 * mixer(h, cos, sin, w_in[l], conv_w[l], conv_b[l], conv_ln_g[l], conv_ln_b[l],
                              w_conv_out[l], b_conv_out[l], q_norm_g[l], k_norm_g[l],
                              lambda_q1[l], lambda_k1[l], lambda_q2[l], lambda_k2[l], lam_init,
                              subln_g[l], w_attn_out[l], b_gate[l], w_o[l])
        h = rms_norm(x, norm2_g[l]) * (1.0 + scale2) + shift2
        x = x + gate2 * moe(h, w_router[l], b_router[l], w_up[l], b_up[l], w_down[l], b_down[l])
    return x


_drawn_inputs = setup_inputs


def setup_inputs(seed=0):
    import zlib

    import numpy as np

    out = dict(_drawn_inputs(seed))
    spreads = {}
    factors = {'conv_b': 6.231,
     'conv_ln_g': 3.539,
     'conv_ln_b': 8.0,
     'b_conv_out': 6.887,
     'q_norm_g': 4.637,
     'k_norm_g': 5.349,
     'lambda_q1': 6.327,
     'lambda_k1': 8.0,
     'lambda_q2': 6.476,
     'lambda_k2': 8.0,
     'subln_g': 2.964,
     'b_gate': 8.0,
     'b_router': 4.571,
     'b_up': 8.0,
     'b_down': 8.0}
    for name, (base, spread) in spreads.items():
        noise = np.random.default_rng([zlib.crc32(name.encode()), seed]).standard_normal(out[name].shape)
        drawn = base * np.exp(spread * noise) if base else spread * noise
        out[name] = __import__('jax').numpy.asarray(drawn.astype(out[name].dtype))
    for name, factor in factors.items():
        out[name] = (out[name] * factor).astype(out[name].dtype)
    return out
```

```python
from contextlib import ExitStack

import concourse.bass as bass
from concourse import mybir

F32 = mybir.dt.float32
BF16 = mybir.dt.bfloat16
I32 = mybir.dt.int32
U32 = mybir.dt.uint32
ALU = mybir.AluOpType
ACT = mybir.ActivationFunctionType
AX = mybir.AxisListType.X

P = 128
T = 256
TT = T // P
D = 1024
KD = D // P
NB = 512
HEADS = 8
HD = 64
VD = 128
ROT = 16
HALF = ROT // 2
THETA = 500000.0
TAPS = 31
PAD = TAPS - 1
EXPERTS = 32
TOPK = 4
SLOTS = 64
UCOLS = 64
EPS = 1e-6
PARTS = 5
MEAN_AT, VAR_AT = 2, 4
ALPHA = 1.702
LIMIT = 7.0
LAM_INIT = 0.2
SUBLN = 1.0 - LAM_INIT
BLOCKF = KD * NB
RING = 6
NSLOT = 12
SLOTF = 2 * D
MASKED = -1e30
UNROUTED = -4096.0
TWO_PI = 6.283185307179586
TWO_PI_HI = 6.28125
TWO_PI_MID = 0.0019350051879882812
TWO_PI_LO = 3.0199159819567e-07
ROUND = 12582912.0
PI_F = 3.1415925


def build(nc, x, c, positions, w_ada, b_ada, norm1_g, w_in, conv_w, conv_b, conv_ln_g, conv_ln_b,
          w_conv_out, b_conv_out, q_norm_g, k_norm_g, lambda_q1, lambda_k1, lambda_q2, lambda_k2,
          subln_g, w_attn_out, b_gate, w_o, norm2_g, w_router, b_router, w_up, b_up, w_down, b_down, out):
    ctx = ExitStack()
    with ctx:
        def sb(name, shape, dt=F32):
            return ctx.enter_context(nc.sbuf_tensor(name, shape, dt))

        def sem(name):
            return ctx.enter_context(nc.semaphore(name))

        W = sb("weights", [P, RING * BLOCKF])
        x_tok = sb("x_tok", [P, TT, D])
        buf_c = sb("buf_c", [P, TT, D])
        buf_d = sb("buf_d", [P, KD, T])
        u_conv = sb("u_conv", [P, KD, PAD + T])
        conv_acc = sb("conv_acc", [P, KD, T])
        buf_k = sb("buf_k", [P, TT, D])
        qkT = sb("qkT", [P, 2, HEADS, T])
        v_tok = sb("v_tok", [P, TT, D])
        gates = sb("gates", [P, TT, 2 * D])

        h1, q_tok = buf_c, buf_c
        oT = buf_c[:, :, :].rearrange("p a b -> p (a b)").rearrange("p (k t) -> p k t", k=KD)
        h1T, mixT = buf_d, buf_d
        k_tok, o_tok = buf_k, buf_k
        qT, kT = qkT[:, 0, :, :], qkT[:, 1, :, :]
        sg_conv = qkT[:, 0, 0:2, :]
        modb = qkT[:, :, :, :].rearrange("p a b c -> p (a b c)").rearrange("p (m d) -> p m d", m=4)
        flat_c = buf_c[:, :, :].rearrange("p a b -> p (a b)")
        pr = flat_c[:, 0:1536].rearrange("p (h c k) -> p h c k", h=2, c=2)
        pa = flat_c[:, 1536:1920]
        norm2_b = buf_c[:, 1, :]
        combT, rankT, routedT = (buf_k[0:EXPERTS, 1, T * i:T * i + T] for i in range(3))
        early = gates[:, :, :].rearrange("p a b -> p (a b)")
        ada_bias = early[:, 0:3 * NB].rearrange("p (g n) -> p g n", g=3)
        g1_rows = early[:, 3 * NB:4 * NB]
        convw_rows = early[0:TAPS, 4 * NB:6 * NB]
        col_rows = early[0:32, 6 * NB:6 * NB + P]
        lam_in = early[:, 3200:3456].rearrange("p (i e) -> p i e", i=4)
        qk_g = early[:, 3456:3584].rearrange("p (i e) -> p i e", i=2)
        rot = early[:, 3584:3840].rearrange("p (i g j) -> p i g j", i=4, g=8)
        rope = early[:, 3840:3968].rearrange("p (i t j) -> p i t j", i=8, t=TT)
        qk_sq = early[:, 4 * NB:5 * NB]
        h2 = gates[:, 0, :].rearrange("p (t d) -> p t d", t=TT)
        h2T = gates[:, 1, :].rearrange("p (k t) -> p k t", k=KD)
        area_q = buf_d[:, :, :].rearrange("p a b -> p (a b)")
        area_k = u_conv[:, :, :].rearrange("p a b -> p (a b)")
        area_v = v_tok[:, :, :].rearrange("p a b -> p (a b)")
        xgT = area_q[:, 0:KD * SLOTS].rearrange("p (k s) -> p k s", k=KD)
        act = area_q[:, 512:1024].rearrange("p (a f) -> p a f", a=2)
        actT = area_q[:, 1024:1536].rearrange("p (a j s) -> p a j s", a=2, j=2)
        oe = area_q[:, 1536:2048]
        Cmb = area_k[:, 0:T]
        pick = area_k[:, 256:256 + TT * SLOTS // 2].bitcast(BF16).rearrange("p (t s) -> p t s", t=TT)
        pickw = area_k[:, 384:384 + TT * P].rearrange("p (t s) -> p t s", t=TT)
        sel = area_k[0:3 * EXPERTS, 640:640 + SLOTS // 2].bitcast(BF16)
        glu = area_k[:, 768:1024]
        lin = area_k[:, 1024:1280]
        sg = area_k[:, 1280:1536]
        gl = area_k[:, 1536:1792]
        ebias = area_v[0:3 * EXPERTS, 0:3 * D // 2].bitcast(BF16)
        ebias_f, ebias_r = buf_k[0:3 * EXPERTS, 0, :], buf_k[0:3 * EXPERTS, 1, :]
        h2_parts = [a.bitcast(BF16).rearrange("p (t d) -> p t d", t=TT) for a in (buf_c[:, 0, :], modb[:, 0, :], modb[:, 1, :])]
        h2_rest = buf_d[:, :, :].rearrange("p a b -> p (a b)").rearrange("p (t d) -> p t d", t=TT)
        wr = conv_acc[:, 4, :].rearrange("p (k e) -> p k e", k=KD)

        qk_junk = sb("qk_junk", [P, T])
        modrow2 = sb("modrow2", [P, 2, NB])
        modrow = modrow2[:, 0, :]
        bias_f = v_tok[0:96, 0, 0:NB]
        bias_b = sb("bias_b", [96, NB], BF16)
        bsel = sb("bsel", [96, 6, P], BF16)
        ln_std = sb("ln_std", [P, T])
        rowsel = sb("rowsel", [P, 4, P])
        ident = sb("ident", [P, P])
        identb = sb("identb", [P, P], BF16)
        zero_b = modb[:, 2, 0:NB // 2].bitcast(BF16)
        maskb = sb("maskb", [P, 3 * P], BF16)
        ones = sb("ones", [P, P])
        upper = sb("upper", [P, TT, T])
        cT = sb("cT", [P, KD])
        c_sig = sb("c_sig", [P, KD])
        c_act = sb("c_act", [P, KD, 32])
        convw = sb("convw", [P, KD, 32])
        cols = sb("cols", [P, 32])
        lam = sb("lam", [P, 8])
        pos_i = sb("pos_i", [P, TT], I32)
        pos_f = sb("pos_f", [P, TT])
        inv_f = sb("inv_f", [P, HALF])
        eps = sb("eps", [P, 1])
        ssq = sb("ssq", [P, 16])
        rstd = sb("rstd", [P, 16])
        qk_ss = sb("qk_ss", [P, 2, 8])
        aT = sb("aT", [P, 384])
        smax = sb("smax", [P, 2, 4])
        ssum = sb("ssum", [P, 2, 4])
        srec = sb("srec", [P, 4])
        br_b = sb("br_b", [P, EXPERTS])
        lg = area_k[:, 320:384].rearrange("p (t e) -> p t e", t=TT)
        top = sb("top", [P, TT, 8])
        topi = sb("topi", [P, TT, 8], U32)
        topf = sb("topf", [P, TT, 8])
        tw = sb("tw", [P, TT, 8])
        comb = sb("comb", [P, TT, EXPERTS])
        comb4 = area_k[:, 672:736].rearrange("p (t e) -> p t e", t=TT)
        routed = sb("routed", [P, TT, EXPERTS])
        iota_e = sb("iota_e", [P, UCOLS])
        iota_s = sb("iota_s", [P, 2, SLOTS])
        tri = sb("tri", [EXPERTS, 2, 3, EXPERTS])
        first = sb("first", [EXPERTS, 1])
        ecol = sb("ecol", [3 * EXPERTS, 10])
        onehot = sb("onehot", [3 * EXPERTS, UCOLS])
        ubase, l_end, l_one = (buf_k[0:EXPERTS, 1, 768 + UCOLS * i:768 + UCOLS * i + UCOLS] for i in range(3))
        u_end = buf_k[0:3 * EXPERTS, 1, 960:960 + UCOLS]
        unit_i = sb("unit_i", [1, 3 * UCOLS + 2], I32)
        upos = area_k[:, 1792:1920].rearrange("p (t u) -> p t u", t=TT)
        uwt = area_k[:, 1920:2048].rearrange("p (t u) -> p t u", t=TT)

        PS = [ctx.enter_context(nc.psum_tensor(f"bank{i}", [P, NB], F32)) for i in range(8)]
        UP = [PS[0], PS[1]]
        DOWN, TR = PS[2], PS[3]
        Y = [[PS[4], PS[5]], [PS[6], PS[7]]]

        blk_full = [sem(f"blk_full{i}") for i in range(RING)]
        w_full = [sem(f"w_full{i}") for i in range(NSLOT)]
        w_free = sem("w_free")
        in_c, in_x, in_rows, in_cols, in_small, in_bias, in_norm2, in_moe, in_rowsb, in_eb = (
            sem(n) for n in ("in_c", "in_x", "in_rows", "in_cols", "in_small", "in_bias", "in_norm2", "in_moe", "in_rowsb", "in_eb"))
        made = sem("constants_made")
        zeroed = sem("bias_rows_zeroed")
        c_ready, ada_done, modrow_ready, bc_done, bc_read = (
            sem(n) for n in ("c_ready", "ada_done", "modrow_ready", "bc_done", "bc_read"))
        h1_ready, h1T_ready, colsT_done, cols_ready = (
            sem(n) for n in ("h1_ready", "h1T_ready", "colsT_done", "cols_ready"))
        bank_full = [sem(f"bank_full{i}") for i in range(4)]
        bank_free = [sem(f"bank_free{i}") for i in range(4)]
        glu_sig, qk_ready, rope_ready, rope_arg = (sem(n) for n in ("glu_sig", "qk_ready", "rope_ready", "rope_arg"))
        act_step, dve_step, x_ssq = sem("act_step"), sem("dve_step"), sem("x_ssq")
        sc_full, s_max, exp_done, pa_ready, aT_ready, o_ready, v_ready = (
            sem(n) for n in ("sc_full", "s_max", "exp_done", "pa_ready", "aT_ready", "o_ready", "v_ready"))
        qkT_ready, modb_ready, on_ready, oT_ready, lam_arg = (
            sem(n) for n in ("qkT_ready", "modb_ready", "on_ready", "oT_ready", "lam_arg"))
        conv_done, cent_ready, csq_ready, var_std, ln_ready, sw_sig, swish_ready = (
            sem(n) for n in ("conv_done", "cent_ready", "csq_ready", "var_std", "ln_ready", "sw_sig", "swish_ready"))
        gate_ready, mixed, y_gated, x1_ready, h2_ready = (
            sem(n) for n in ("gate_ready", "mixed", "y_gated", "x1_ready", "h2_ready"))
        lg_ready, tw_ready, routed_ready, tr_done, cnt_ready, m_ready, end_done, oh_ready, units_done, units_ready = (
            sem(n) for n in ("lg_ready", "tw_ready", "routed_ready", "tr_done", "cnt_ready", "m_ready", "end_done",
                             "oh_ready", "units_done", "units_ready"))
        mod_ready, ebias_ready, h2_split, bias_step = (
            sem(n) for n in ("mod_ready", "ebias_ready", "h2_split", "bias_step"))
        pick_ready, pickw_ready, sel_ready, gathered, xg_ready = (
            sem(n) for n in ("pick_ready", "pickw_ready", "sel_ready", "gathered", "xg_ready"))
        up_done = [sem("up0_done"), sem("up1_done")]
        glu_ready = [sem("glu0_ready"), sem("glu1_ready")]
        sg_ready = [sem("sg0_ready"), sem("sg1_ready")]
        act_ready = [sem("act0_ready"), sem("act1_ready")]
        t_done = [sem("t0_done"), sem("t1_done")]
        actT_ready = [sem("actT0_ready"), sem("actT1_ready")]
        ct_done, cmb_ready, down_done, oe_ready, combined = (
            sem(n) for n in ("ct_done", "cmb_ready", "down_done", "oe_ready", "combined"))
        out_ready, stored, u_step = sem("out_ready"), sem("stored"), sem("u_step")

        def block_of(w, col):
            return w[0, :, col:col + NB].rearrange("(k p) n -> p k n", p=P)

        def ada_block(col):
            return w_ada[0, :, col:col + NB].rearrange("(p k) n -> p k n", k=KD)

        blocks = [ada_block(NB * i) for i in range(4)]
        CONV0 = len(blocks)
        for i in (0, 2, 1, 3):
            blocks.append(block_of(w_in, NB * i))
        QKV0 = len(blocks)
        blocks += [block_of(w_in, NB * i) for i in range(4, 10)]
        ADA1 = len(blocks)
        blocks += [ada_block(NB * i) for i in range(4, 12)]
        GATE0 = len(blocks)
        blocks += [block_of(w_in, NB * i) for i in range(10, 14)]
        AOUT0 = len(blocks)
        blocks += [block_of(w_attn_out, 0), block_of(w_attn_out, NB)]
        COUT0 = len(blocks)
        blocks += [block_of(w_conv_out, 0), block_of(w_conv_out, NB)]
        WO0 = len(blocks)
        blocks += [block_of(w_o, 0), block_of(w_o, NB)]
        SHIFT = (RING - len(blocks)) % RING

        def place(n):
            return (n + SHIFT) % RING

        def blk(n):
            return W[:, place(n) * BLOCKF:(place(n) + 1) * BLOCKF].rearrange("p (k n) -> p k n", k=KD)

        loads_before = [sum(place(m) == place(n) for m in range(n + 1)) for n in range(len(blocks))]
        used = {}

        def used_by(n, use):
            used[n] = (bank_full[use % 4], use // 4 + 1)

        def wslot(i):
            return W[:, i * SLOTF:(i + 1) * SLOTF].rearrange("p (k n) -> p k n", k=2)

        order = [("h1T", i) for i in range(4)] + [("conv", i) for i in range(8)]
        order += [("qk", i) for i in range(8)] + [("v", i) for i in range(4)] + [("qkT", i) for i in range(8)]
        order += [("ada", 0), ("ada", 1)]
        for h in range(HEADS + 1):
            if h < HEADS:
                order += [("gate", h)]
            if h:
                order += [("aT", h - 1), ("o", h - 1)]
            if h == MEAN_AT:
                order += [("mean", 0)]
            if h == VAR_AT:
                order += [("var", 0)]
        order += [(name, i) for name in ("oT", "y_attn", "y_conv", "mixT", "w_o", "h2T") for i in range(4)]
        order += [(name, 0) for name in ("logits", "routing", "counts", "ends", "units")]
        use_of = {what: n for n, what in enumerate(order)}

        HT_USE = use_of["h1T", 0]
        CONV_USE = use_of["conv", 0]
        QK_USE = use_of["qk", 0]
        V_USE = use_of["v", 0]
        QKT_USE = use_of["qkT", 0]
        ADA_USE = use_of["ada", 0]
        YC_USE = use_of["y_conv", 0]
        OT_USE = use_of["oT", 0]
        YA_USE = use_of["y_attn", 0]
        MT_USE = use_of["mixT", 0]
        WO_USE = use_of["w_o", 0]
        H2T_USE = use_of["h2T", 0]
        LG_USE = use_of["logits", 0]
        RT_USE = use_of["routing", 0]
        CNT_USE = use_of["counts", 0]
        END_USE = use_of["ends", 0]
        UN_USE = use_of["units", 0]
        MEAN_USE, VAR_USE = use_of["mean", 0], use_of["var", 0]

        def gate_use(h):
            return use_of["gate", h]

        def aT_use(h):
            return use_of["aT", h]

        def o_use(h):
            return use_of["o", h]

        for i in range(4):
            used[i] = (ada_done, i + 1)
            used_by(CONV0 + i, CONV_USE + 3 + 4 * (i // 2))
            used_by(QKV0 + i, QK_USE + 2 * i + 1)
            used_by(GATE0 + i, gate_use(2 * i + 1))
            for gi in range(2):
                used[ADA1 + 4 * gi + i] = (ada_done, 4 + 3 * gi + i + 1)
        for i in range(2):
            used_by(ADA1 + 4 * i + 3, ADA_USE + i)
            used_by(QKV0 + 4 + i, V_USE + 2 * i + 1)
            used_by(COUT0 + i, YC_USE + 2 * i + 1)
            used_by(AOUT0 + i, YA_USE + 2 * i + 1)
            used_by(WO0 + i, WO_USE + 2 + i)

        def bank(use):
            return PS[use % 4]

        def full(eng, use):
            eng.wait_ge(bank_full[use % 4], use // 4 + 1)

        def fill(pe, use):
            if use >= 4:
                pe.wait_ge(bank_free[use % 4], use // 4)

        block = ctx.enter_context(nc.Block())

        @block.sync
        def _(sp):
            sp.dma_start(cT[:], c.rearrange("b (p k) -> p (b k)", k=KD)).then_inc(in_c, 16)
            sp.dma_start(x_tok[:], x[0].rearrange("(t p) d -> p t d", p=P)).then_inc(in_x, 16)
            for gi in range(4):
                sp.dma_start(ada_bias[32 * gi:32 * gi + 32, :, :],
                             b_ada[0:1, :].rearrange("o (g i n) -> o g i n", g=3, i=4)[:, :, gi, :].to_broadcast(
                                 [32, 3, NB])).then_inc(in_rows, 16)
            for gi in range(2):
                sp.dma_start(g1_rows[64 + 32 * gi:96 + 32 * gi, :],
                             norm1_g[0:1, gi * NB:(gi + 1) * NB].to_broadcast([32, NB])).then_inc(in_rows, 16)
            for n, src in enumerate(blocks):
                if n >= RING:
                    sp.wait_ge(*used[n - RING])
                sp.dma_start(blk(n), src).then_inc(blk_full[place(n)], 16)

            def load_unit(e, wait):
                for i in range(NSLOT):
                    wait(i)
                    pair = 2 * P * (i % 4)
                    if i < 8:
                        col = D * (i // 4)
                        src = w_up[0, e, pair:pair + 2 * P, col:col + D]
                    else:
                        src = w_down[0, e, pair:pair + 2 * P, :]
                    if not isinstance(e, int):
                        src = src.rearrange("o a n -> (o a) n")
                    sp.dma_start(wslot(i), src.rearrange("(k p) n -> p k n", p=P)).then_inc(w_full[i], 16)

            load_unit(0, lambda i: sp.wait_ge(*used[len(blocks) - RING + i // 2]))
            sp.wait_ge(units_ready, 1)
            loads = sp.value_load(unit_i[0:1, 3 * UCOLS + 1:3 * UCOLS + 2], min_val=TOPK, max_val=EXPERTS)
            with sp.Fori(1, loads) as n:
                e = sp.value_load(unit_i[0:1, bass.ds(n + UCOLS, 1)], min_val=0, max_val=EXPERTS - 1)
                before = sp.value_load(unit_i[0:1, bass.ds(n + 2 * UCOLS, 1)], min_val=0, max_val=46)

                def slot_used(i):
                    if i % 4 == 3:
                        sp.wait_ge((up_done[0], up_done[1], down_done)[i // 4], before + 1)
                    else:
                        sp.wait_ge(w_free, before * 9 + 3 * (i // 4) + i % 4 + 1)

                load_unit(bass.ds(e, 1), slot_used)
            for tt in range(TT):
                sp.wait_ge(out_ready, 2 * tt + 2)
                sp.dma_start(out[0, tt * P:(tt + 1) * P, :], x_tok[:, tt, :]).then_inc(stored, 16)
            sp.wait_ge(stored, 32)

        @block.gpsimd
        def _(pool):
            g = nc.gpsimd
            n = 0

            def step(ins):
                nonlocal n
                n += 1
                ins.then_inc(made, 1)
                pool.wait_ge(made, n)

            step(g.memset(ones[:], 1.0))
            step(g.memset(rowsel[:], 0.0))
            for gi in range(4):
                step(g.affine_select(out=rowsel[:, gi, :], in_=ones[:], pattern=[[0, P]], base=-32 * gi,
                                     channel_multiplier=1, compare_op=ALU.is_equal, fill=0.0))
            step(g.affine_select(out=ident[:], in_=ones[:], pattern=[[-1, P]], base=0, channel_multiplier=1,
                                 compare_op=ALU.is_equal, fill=0.0))
            step(g.tensor_copy(identb[:], ident[:]))
            step(g.memset(maskb[:], 0.0))
            for o in (0, 2 * P):
                step(g.affine_select(out=maskb[:, o:o + P], in_=maskb[:, o:o + P], pattern=[[-1, P]], base=0,
                                     channel_multiplier=1, compare_op=ALU.is_ge, fill=MASKED))
            step(g.memset(upper[:], 1.0))
            for tt in range(TT):
                step(g.affine_select(out=upper[:, tt, :], in_=upper[:, tt, :], pattern=[[1, T]], base=-P * tt,
                                     channel_multiplier=-1, compare_op=ALU.is_gt, fill=0.0))
            step(g.memset(tri[:], 1.0))
            for i, op in enumerate((ALU.is_ge, ALU.is_gt)):
                step(g.affine_select(out=tri[:, i, :, :], in_=tri[:, i, :, :], pattern=[[0, 3], [1, EXPERTS]], base=0,
                                     channel_multiplier=-1, compare_op=op, fill=0.0))
            step(g.memset(bsel[:], 1.0))
            for q in range(3):
                step(g.affine_select(out=bsel[32 * q:32 * q + 32, :, :], in_=bsel[32 * q:32 * q + 32, :, :],
                                     pattern=[[-1, 6], [0, P]], base=0, channel_multiplier=1,
                                     compare_op=ALU.is_equal, fill=0.0))
            step(g.affine_select(out=first[:], in_=ones[0:EXPERTS, 0:1], pattern=[[0, 1]], base=0,
                                 channel_multiplier=1, compare_op=ALU.is_equal, fill=0.0))
            step(g.iota(iota_e[:], pattern=[[1, UCOLS]], base=0, channel_multiplier=0,
                        allow_small_or_imprecise_dtypes=True))
            step(g.iota(iota_s[:], pattern=[[0, 2], [1, SLOTS]], base=0, channel_multiplier=0,
                        allow_small_or_imprecise_dtypes=True))
            for j in range(HALF):
                step(g.memset(inv_f[:, j:j + 1], float(THETA ** (-2.0 * j / ROT))))
            step(g.memset(u_conv[:, :, 0:PAD], 0.0))
            pool.wait_ge(in_rowsb, 16 * 6)
            m = 0

            def part(ins, sem_, n):
                ins.then_inc(sem_, 1)
                pool.wait_ge(sem_, n)

            def parts(dst, src, rest, sem_, n):
                part(g.tensor_copy(dst[0:96, :], src[0:96, :]), sem_, n + 1)
                part(g.tensor_tensor(rest[0:96, :], src[0:96, :], dst[0:96, :], ALU.subtract), sem_, n + 2)
                for q in (1, 2):
                    rows = slice(32 * q, 32 * q + 32)
                    part(g.tensor_copy(dst[rows, :], rest[rows, :]), sem_, n + 2 + q)
                part(g.tensor_tensor(dst[64:96, :], rest[64:96, :], dst[64:96, :], ALU.subtract), sem_, n + PARTS)

            parts(bias_b, bias_f, bias_f, bias_step, 0)
            for gi in range(2):
                pool.wait_ge(bank_free[(ADA_USE + gi) % 4], (ADA_USE + gi) // 4 + 1)
            pool.wait_ge(sc_full, HEADS)
            for gi in range(4):
                for q in range(4):
                    pool.dma_start(modb[32 * q:32 * q + 32, gi // 2:4:2, NB * (gi % 2):NB * (gi % 2) + NB],
                                   modrow2[32 * gi:32 * gi + 32, :, :]).then_inc(mod_ready, 16)
            for i in range(4):
                pool.wait_ge(bank_full[(OT_USE + i) % 4], (OT_USE + i) // 4 + 1)
            for piece in range(3):
                src = b_up[0, :, D * piece:D * piece + D] if piece < 2 else b_down[0]
                dst = ebias[:, D * piece:D * piece + D]
                for q in range(3):
                    pool.dma_start(ebias_f[32 * q:32 * q + 32, :], src).then_inc(in_eb, 16)
                pool.wait_ge(in_eb, 48 * (piece + 1))
                parts(dst, ebias_f, ebias_r, ebias_ready, PARTS * piece)
            pool.wait_ge(h2_ready, TT)
            part(g.tensor_copy(h2_parts[0], h2), h2_split, 1)
            part(g.tensor_tensor(h2_rest, h2, h2_parts[0], ALU.subtract), h2_split, 2)
            part(g.tensor_copy(h2_parts[1], h2_rest), h2_split, 3)
            part(g.tensor_tensor(h2_parts[2], h2_rest, h2_parts[1], ALU.subtract), h2_split, 4)

        MADE = 1 + 1 + 4 + 1 + 1 + 1 + 2 + 1 + TT + (1 + 2) + (1 + 3) + 1 + 1 + 1 + HALF + 1

        @block.scalar
        def _(act_e):
            s = nc.scalar

            def load(dst, src, into):
                act_e.dma_start(dst, src).then_inc(into, 16)

            act_e.wait_ge(zeroed, 1)
            load(convw_rows, conv_w[0], in_cols)
            for i, w in enumerate((conv_b, conv_ln_g, conv_ln_b)):
                load(col_rows[8 * i:8 * i + 8, :], w[0].rearrange("(k p) -> k p", p=P), in_cols)
            load(col_rows[24:25, :], subln_g, in_cols)
            for i, w in enumerate((lambda_q1, lambda_k1, lambda_q2, lambda_k2)):
                load(lam_in[:, i, :], w.to_broadcast([P, HD]), in_small)
            for i, w in enumerate((q_norm_g, k_norm_g)):
                load(qk_g[:, i, :], w.to_broadcast([P, HD]), in_small)
            for tt in range(TT):
                load(pos_i[:, tt:tt + 1], positions[0, tt * P:(tt + 1) * P].rearrange("(p o) -> p o", o=1), in_small)
            load(br_b[:], b_router.to_broadcast([P, EXPERTS]), in_bias)
            for q in range(3):
                load(bias_f[32 * q:32 * q + 4, :], b_gate[0].rearrange("(i n) -> i n", n=NB), in_rowsb)
                load(bias_f[32 * q + 4:32 * q + 6, :], b_conv_out[0].rearrange("(i n) -> i n", n=NB), in_rowsb)

            act_e.wait_ge(in_c, 16)
            s.activation(c_sig[:], cT[:], ACT.Sigmoid).then_inc(act_step, 1)
            act_e.wait_ge(in_x, 16)
            for tt in range(TT):
                s.activation(buf_k[:, tt, :], x_tok[:, tt, :], ACT.Square, accum_out=ssq[:, tt:tt + 1]).then_inc(x_ssq, 1)
            act_e.wait_ge(x_ssq, TT)
            act_e.wait_ge(zeroed, 1)
            s.activation(rstd[:, 0:TT], ssq[:, 0:TT], ACT.Sqrt, scale=1.0 / D, bias=eps[:]).then_inc(x_ssq, 1)
            act_e.wait_ge(rope_arg, 1)
            s.activation(rope[:, 6:8, :, :].rearrange("p a t j -> p (a t j)"),
                         rope[:, 4:6, :, :].rearrange("p a t j -> p (a t j)"), ACT.Sin).then_inc(rope_ready, 1)
            act_e.wait_ge(lam_arg, 1)
            s.activation(lam[:, 2:4], lam[:, 0:2], ACT.Exp).then_inc(lam_arg, 1)
            for i in range(4):
                full(act_e, HT_USE + i)
                s.copy(h1T[:, 4 * (i % 2):4 * (i % 2) + 4, P * (i // 2):P * (i // 2) + P],
                       bank(HT_USE + i)[:, :].rearrange("p (k t) -> p k t", k=4)).then_inc(bank_free[(HT_USE + i) % 4], 1)
            for k in range(KD):
                full(act_e, CONV_USE + k)
                if k >= 2:
                    act_e.wait_ge(bank_free[(CONV_USE + k - 2) % 4], (CONV_USE + k - 2) // 4 + 1)
                s.activation(sg_conv[:, k % 2, :], bank(CONV_USE + k)[:, T:2 * T], ACT.Sigmoid).then_inc(glu_sig, 1)
            for i in range(8):
                full(act_e, QK_USE + i)
                if i:
                    act_e.wait_ge(qk_ready, 2 * i - 1)
                s.activation(qk_sq, bank(QK_USE + i)[:, :], ACT.Square).then_inc(glu_sig, 1)
                act_e.wait_ge(qk_ready, 2 * i + 1)
                s.activation(qk_ss[:, 1, :], qk_ss[:, 0, :], ACT.Sqrt, scale=1.0 / HD, bias=eps[:]).then_inc(glu_sig, 1)
            act_e.wait_ge(bias_step, PARTS)
            for i in range(4):
                full(act_e, V_USE + i)
                s.copy(v_tok[:, i % 2, NB * (i // 2):NB * (i // 2) + NB], bank(V_USE + i)[:, :]).then_inc(
                    bank_free[(V_USE + i) % 4], 1)
            for i in range(8):
                full(act_e, QKT_USE + i)
                dst = (qT if i < 4 else kT)[:, 2 * (i % 4):2 * (i % 4) + 2, :]
                s.copy(dst, bank(QKT_USE + i)[:, :].rearrange("p (h t) -> p h t", h=2)).then_inc(
                    bank_free[(QKT_USE + i) % 4], 1)

            def attended(h):
                use = aT_use(h)
                full(act_e, use)
                s.copy(aT[:], bank(use)[:, 0:384]).then_inc(bank_free[use % 4], 1)
                use = o_use(h)
                full(act_e, use)
                for tt in range(TT):
                    s.activation(qk_junk[:, P * tt:P * tt + P], bank(use)[:, P * tt:P * tt + P], ACT.Square,
                                 accum_out=ssq[:, tt * 8 + h:tt * 8 + h + 1]).then_inc(o_ready, 1)

            for h in range(HEADS):
                par = h % 2
                act_e.wait_ge(s_max, h + 1)
                for part in range(2):
                    sc = PS[4 + 2 * par + part]
                    for blk_q, (a, b) in enumerate(((0, P), (P, 3 * P))):
                        at = 2 * blk_q + part
                        s.activation(pr[:, par, part, a:b], sc[:, a:b], ACT.Exp, scale=HD ** -0.5,
                                     bias=smax[:, par, at:at + 1], accum_out=ssum[:, par, at:at + 1]).then_inc(exp_done, 1)
                use = gate_use(h)
                full(act_e, use)
                s.copy(gates[:, h % 2, NB * (h // 2):NB * (h // 2) + NB], bank(use)[:, :]).then_inc(bank_free[use % 4], 1)
                if h:
                    attended(h - 1)
                if h == MEAN_AT + 1:
                    act_e.wait_ge(bank_free[MEAN_USE % 4], MEAN_USE // 4 + 1)
                    s.activation(u_conv[:, :, 0:T], conv_acc[:], ACT.Square).then_inc(csq_ready, 1)
                if h == VAR_AT:
                    full(act_e, VAR_USE)
                    s.copy(ln_std[:], bank(VAR_USE)[:, 0:T]).then_inc(bank_free[VAR_USE % 4], 1)
            attended(HEADS - 1)
            act_e.wait_ge(o_ready, 2 * HEADS)
            s.activation(rstd[:], ssq[:], ACT.Sqrt, scale=1.0 / VD, bias=eps[:]).then_inc(o_ready, 1)
            act_e.wait_ge(bank_free[VAR_USE % 4], VAR_USE // 4 + 1)
            s.activation(ln_std[:], ln_std[:], ACT.Sqrt, scale=1.0 / D, bias=eps[:]).then_inc(var_std, 1)
            for tt in range(TT):
                s.activation(gates[:, tt, :], gates[:, tt, :], ACT.Sigmoid).then_inc(gate_ready, 1)
            for i in range(4):
                full(act_e, OT_USE + i)
                s.activation(oT[:, 4 * (i % 2):4 * (i % 2) + 4, P * (i // 2):P * (i // 2) + P],
                             bank(OT_USE + i)[:, :].rearrange("p (k t) -> p k t", k=4), ACT.Copy,
                             scale=cols[:, 25:26]).then_inc(bank_free[(OT_USE + i) % 4], 1)
            act_e.wait_ge(ln_ready, 1)
            for k in range(KD):
                s.activation(u_conv[:, k, 0:T], conv_acc[:, k, :], ACT.Sigmoid, scale=cols[:, 8 + k:9 + k],
                             bias=cols[:, 16 + k:17 + k]).then_inc(sw_sig, 1)
            for i in range(4):
                full(act_e, MT_USE + i)
                s.copy(mixT[:, 4 * (i % 2):4 * (i % 2) + 4, P * (i // 2):P * (i // 2) + P],
                       bank(MT_USE + i)[:, :].rearrange("p (k t) -> p k t", k=4)).then_inc(bank_free[(MT_USE + i) % 4], 1)
            load(wr, w_router[0].rearrange("(k p) e -> p k e", p=P), in_moe)
            load(norm2_b, norm2_g.to_broadcast([P, D]), in_norm2)
            for tt in range(TT):
                act_e.wait_ge(x1_ready, 2 * tt + 2)
                s.activation(gates[:, tt, D:2 * D], x_tok[:, tt, :], ACT.Square, accum_out=ssq[:, tt:tt + 1]).then_inc(x_ssq, 1)
            act_e.wait_ge(x_ssq, TT + 1 + TT)
            s.activation(rstd[:, 0:TT], ssq[:, 0:TT], ACT.Sqrt, scale=1.0 / D, bias=eps[:]).then_inc(x_ssq, 1)
            for i in range(4):
                full(act_e, H2T_USE + i)
                s.copy(h2T[:, 4 * (i % 2):4 * (i % 2) + 4, P * (i // 2):P * (i // 2) + P],
                       bank(H2T_USE + i)[:, :].rearrange("p (k t) -> p k t", k=4)).then_inc(bank_free[(H2T_USE + i) % 4], 1)
            act_e.wait_ge(lg_ready, 1)
            for tt in range(TT):
                s.activation(tw[:, tt, 0:TOPK], topf[:, tt, 0:TOPK], ACT.Exp, accum_out=tw[:, tt, 4:5]).then_inc(tw_ready, 1)

            act_e.wait_ge(units_ready, 2)
            count = act_e.value_load(unit_i[0:1, 3 * UCOLS:3 * UCOLS + 1], min_val=TOPK, max_val=47)
            act_e.wait_ge(gathered, 1)
            s.copy(xgT, UP[0][:, :].rearrange("p (k s) -> p k s", k=KD)).then_inc(xg_ready, 1)
            with act_e.Fori(0, count) as u:
                def keep_act(a):
                    act_e.wait_ge(t_done[a], u + 1)
                    s.copy(actT[:, a, :, :], TR[:, T * a:T * a + T].rearrange("p (j s) -> p j s", j=2)).then_inc(
                        actT_ready[a], 1)

                act_e.wait_ge(glu_ready[0], u + 1)
                s.activation(sg, glu, ACT.Sigmoid, scale=ALPHA).then_inc(sg_ready[0], 1)
                keep_act(0)
                act_e.wait_ge(glu_ready[1], u + 1)
                s.activation(sg, glu, ACT.Sigmoid, scale=ALPHA).then_inc(sg_ready[1], 1)
                act_e.wait_ge(gathered, u + 2)
                s.copy(xgT, UP[0][:, :].rearrange("p (k s) -> p k s", k=KD)).then_inc(xg_ready, 1)
                keep_act(1)
                act_e.wait_ge(ct_done, u + 1)
                s.copy(Cmb, TR[:, 0:T]).then_inc(cmb_ready, 1)
                act_e.wait_ge(down_done, u + 1)
                s.copy(oe, DOWN[:, :]).then_inc(oe_ready, 1)

        @block.vector
        def _(dve):
            v = nc.vector
            n = 0

            def step(ins):
                nonlocal n
                n += 1
                ins.then_inc(dve_step, 1)
                dve.wait_ge(dve_step, n)

            step(v.memset(eps[:], EPS))
            step(v.memset(bias_f, 0.0))
            v.memset(col_rows, 0.0).then_inc(zeroed, 1)
            dve.wait_ge(act_step, 1)
            v.tensor_tensor(c_act[:], c_sig[:].unsqueeze(2).to_broadcast([P, KD, 32]),
                            cT[:].unsqueeze(2).to_broadcast([P, KD, 32]), ALU.mult).then_inc(c_ready, 1)
            dve.wait_ge(x_ssq, TT + 1)
            step(v.reciprocal(rstd[:, 0:TT], rstd[:, 0:TT]))
            dve.wait_ge(in_small, 16 * 8)
            dve.wait_ge(made, MADE)
            step(v.tensor_copy(pos_f[:], pos_i[:]))
            ang = rope[:, 0, :, :]
            for tt in range(TT):
                step(v.tensor_scalar(rope[:, 0, tt, :], inv_f[:], pos_f[:, tt:tt + 1], None, ALU.mult))
            for k, (turn, add) in enumerate(((0.25, TWO_PI / 4), (0.0, 0.0))):
                r, t = rope[:, 4 + k, :, :], rope[:, 1, :, :]
                step(v.tensor_scalar(t, ang, 1.0 / TWO_PI, turn, ALU.mult, ALU.add))
                step(v.tensor_scalar(t, t, ROUND, None, ALU.add))
                step(v.tensor_scalar(t, t, -ROUND, None, ALU.add))
                step(v.scalar_tensor_tensor(r, t, -TWO_PI_HI, ang, ALU.mult, ALU.add))
                step(v.scalar_tensor_tensor(r, t, -TWO_PI_MID, r, ALU.mult, ALU.add))
                step(v.scalar_tensor_tensor(r, t, -TWO_PI_LO, r, ALU.mult, ALU.add))
                step(v.tensor_scalar(r, r, add, None, ALU.add))
                ins = v.tensor_scalar(r, r, PI_F, -PI_F, ALU.min, ALU.max)
                if k == 0:
                    step(ins)
                else:
                    ins.then_inc(rope_arg, 1)
            dve.wait_ge(in_rows, 16 * 6)
            dve.wait_ge(ada_done, 4)
            step(v.tensor_tensor(modrow, PS[4][:, :], ada_bias[:, 0, :], ALU.add))
            v.scalar_tensor_tensor(modrow[64:128, :], modrow[64:128, :], 1.0, g1_rows[64:128, :], ALU.add,
                                   ALU.mult).then_inc(modrow_ready, 1)
            for i in range(2):
                step(v.tensor_tensor(lam_in[:, 2 * i, :], lam_in[:, 2 * i, :], lam_in[:, 2 * i + 1, :], ALU.mult))
                ins = v.tensor_reduce(lam[:, i:i + 1], lam_in[:, 2 * i, :], axis=AX, op=ALU.add)
                if i == 0:
                    step(ins)
                else:
                    ins.then_inc(lam_arg, 1)
            dve.wait_ge(bc_done, 1)
            for tt in range(TT):
                for i in range(2):
                    hs = h1[:, tt, NB * i:NB * i + NB]
                    step(v.scalar_tensor_tensor(hs, x_tok[:, tt, NB * i:NB * i + NB], rstd[:, tt:tt + 1],
                                                PS[6 + i][:, :], ALU.mult, ALU.mult))
                    v.tensor_tensor(hs, hs, PS[4 + i][:, :], ALU.add).then_inc(h1_ready, 1)
            dve.wait_ge(lam_arg, 2)
            step(v.tensor_tensor(lam[:, 4:5], lam[:, 3:4], lam[:, 2:3], ALU.subtract))
            step(v.tensor_scalar(lam[:, 5:6], lam[:, 4:5], -LAM_INIT, None, ALU.add))
            dve.wait_ge(colsT_done, 1)
            step(v.tensor_copy(convw[:, :, 0:TAPS], PS[4][:, 0:KD * TAPS].rearrange("p (k w) -> p k w", k=KD)))
            step(v.tensor_copy(cols[:, 0:25], PS[5][:, 0:25]))
            v.tensor_scalar(cols[:, 25:26], cols[:, 24:25], SUBLN, None, ALU.mult).then_inc(cols_ready, 1)
            dve.wait_ge(cols_ready, 1)

            def glu_tile(k):
                use = CONV_USE + k
                dve.wait_ge(glu_sig, k + 1)
                v.tensor_tensor(u_conv[:, k, PAD:PAD + T], bank(use)[:, 0:T], sg_conv[:, k % 2, :],
                                ALU.mult).then_inc(bank_free[use % 4], 1)

            def conv_tile(k):
                use = CONV_USE + k
                dve.wait_ge(bank_free[use % 4], use // 4 + 1)
                acc = conv_acc[:, k, :]
                step(v.tensor_scalar(acc, u_conv[:, k, 0:T], convw[:, k, 0:1], cols[:, k:k + 1], ALU.mult, ALU.add))
                for w in range(1, TAPS):
                    ins = v.scalar_tensor_tensor(acc, u_conv[:, k, w:w + T], convw[:, k, w:w + 1], acc,
                                                 ALU.mult, ALU.add)
                    if w < TAPS - 1:
                        step(ins)
                    else:
                        ins.then_inc(conv_done, 1)

            for before, k in (((0,), 0), ((1, 2), 1), ((3,), 2), ((4, 5), 3), ((6,), 4), ((7,), 5)):
                for b in before:
                    glu_tile(b)
                conv_tile(k)
            dve.wait_ge(rope_ready, 1)
            for i in range(8):
                use = QK_USE + i
                tt, col, which = i % 2, NB * ((i // 2) % 2), i // 4
                dst = (q_tok, k_tok)[which][:, tt, col:col + NB].rearrange("p (g e) -> p g e", g=8)
                dve.wait_ge(glu_sig, KD + 2 * i + 1)
                v.tensor_reduce(qk_ss[:, 0, :], qk_sq.rearrange("p (g e) -> p g e", g=8), axis=AX,
                                op=ALU.add).then_inc(qk_ready, 1)
                dve.wait_ge(glu_sig, KD + 2 * i + 2)
                step(v.reciprocal(qk_ss[:, 1, :], qk_ss[:, 1, :]))
                if i == 0:
                    dve.wait_ge(bank_full[3], 1)
                v.tensor_tensor(dst, bank(use)[:, :].rearrange("p (g e) -> p g e", g=8),
                                qk_ss[:, 1, :].unsqueeze(2).to_broadcast([P, 8, HD]), ALU.mult).then_inc(bank_free[use % 4], 1)
                dve.wait_ge(bank_free[use % 4], use // 4 + 1)
                step(v.tensor_tensor(dst, dst, qk_g[:, which, :].unsqueeze(1).to_broadcast([P, 8, HD]), ALU.mult))
                cos = rope[:, 6, tt, :].unsqueeze(1).to_broadcast([P, 8, HALF])
                sin = rope[:, 7, tt, :].unsqueeze(1).to_broadcast([P, 8, HALF])
                x1, x2 = dst[:, :, 0:HALF], dst[:, :, HALF:ROT]
                v.tensor_tensor(rot[:, 0, :, :], x1, cos, ALU.mult)
                v.tensor_tensor(rot[:, 1, :, :], x2, sin, ALU.mult)
                v.tensor_tensor(rot[:, 2, :, :], x2, cos, ALU.mult)
                step(v.tensor_tensor(rot[:, 3, :, :], x1, sin, ALU.mult))
                v.tensor_tensor(x1, rot[:, 0, :, :], rot[:, 1, :, :], ALU.subtract)
                v.tensor_tensor(x2, rot[:, 2, :, :], rot[:, 3, :, :], ALU.add).then_inc(qk_ready, 1)
                if i in (4, 7):
                    conv_tile(6 + i // 7)
            for gi in range(2):
                use = ADA_USE + gi
                full(dve, use)
                v.tensor_tensor(modrow2[:, gi, :], bank(use)[:, :], ada_bias[:, 1 + gi, :], ALU.add).then_inc(bank_free[use % 4], 1)

            def keep_o(h):
                use = o_use(h)
                if h == 0:
                    full(dve, QKT_USE + 7)
                dve.wait_ge(o_ready, 2 * h + 2)
                v.tensor_copy(o_tok[:, :, VD * h:VD * h + VD],
                              bank(use)[:, 0:2 * VD].rearrange("p (t e) -> p t e", t=2)).then_inc(bank_free[use % 4], 1)

            for h in range(HEADS):
                par = h % 2
                dve.wait_ge(sc_full, h + 1)
                for blk_q, (a, b) in enumerate(((0, P), (P, 3 * P))):
                    for part in range(2):
                        at = 2 * blk_q + part
                        ins = v.tensor_reduce(smax[:, par, at:at + 1], PS[4 + 2 * par + part][:, a:b], axis=AX, op=ALU.max)
                step(ins)
                v.tensor_scalar(smax[:, par, :], smax[:, par, :], -(HD ** -0.5), None, ALU.mult).then_inc(s_max, 1)
                dve.wait_ge(exp_done, 4 * h + 4)
                step(v.reciprocal(srec[:], ssum[:, par, :]))
                step(v.tensor_scalar(srec[:].rearrange("p (b c) -> p b c", c=2)[:, :, 1],
                                     srec[:].rearrange("p (b c) -> p b c", c=2)[:, :, 1], lam[:, 5:6], None, ALU.mult))
                if h:
                    full(dve, aT_use(h - 1))
                for blk_q, (a, b) in enumerate(((0, P), (P, 3 * P))):
                    step(v.tensor_scalar(pa[:, a:b], pr[:, par, 0, a:b], srec[:, 2 * blk_q:2 * blk_q + 1], None, ALU.mult))
                    ins = v.scalar_tensor_tensor(pa[:, a:b], pr[:, par, 1, a:b], srec[:, 2 * blk_q + 1:2 * blk_q + 2],
                                                 pa[:, a:b], ALU.mult, ALU.add)
                ins.then_inc(pa_ready, 1)
                if h:
                    keep_o(h - 1)
                if h == MEAN_AT:
                    full(dve, MEAN_USE)
                    v.scalar_tensor_tensor(conv_acc[:], bank(MEAN_USE)[:, 0:T].unsqueeze(1).to_broadcast([P, KD, T]),
                                           -1.0 / D, conv_acc[:], ALU.mult, ALU.add).then_inc(bank_free[MEAN_USE % 4], 1)
            keep_o(HEADS - 1)
            dve.wait_ge(o_ready, 2 * HEADS + 1)
            dve.wait_ge(bank_free[o_use(HEADS - 1) % 4], o_use(HEADS - 1) // 4 + 1)
            step(v.reciprocal(rstd[:], rstd[:]))
            v.tensor_tensor(o_tok[:].rearrange("p t (h e) -> p (t h) e", h=HEADS),
                            o_tok[:].rearrange("p t (h e) -> p (t h) e", h=HEADS),
                            rstd[:].unsqueeze(2).to_broadcast([P, 16, VD]), ALU.mult).then_inc(on_ready, 1)
            dve.wait_ge(var_std, 1)
            step(v.reciprocal(ln_std[:], ln_std[:]))
            v.tensor_tensor(conv_acc[:], conv_acc[:], ln_std[:].unsqueeze(1).to_broadcast([P, KD, T]),
                            ALU.mult).then_inc(ln_ready, 1)
            dve.wait_ge(gate_ready, TT)

            def gated_attn(i):
                full(dve, YA_USE + i)
                ga = gates[:, i % 2, D + NB * (i // 2):D + NB * (i // 2) + NB]
                v.tensor_tensor(ga, ga, bank(YA_USE + i)[:, :], ALU.mult).then_inc(bank_free[(YA_USE + i) % 4], 1)

            gated_attn(0)
            for k in range(KD):
                dve.wait_ge(sw_sig, k + 1)
                step(v.tensor_scalar(conv_acc[:, k, :], conv_acc[:, k, :], cols[:, 8 + k:9 + k], cols[:, 16 + k:17 + k],
                                     ALU.mult, ALU.add))
                v.tensor_tensor(conv_acc[:, k, :], conv_acc[:, k, :], u_conv[:, k, 0:T], ALU.mult).then_inc(swish_ready, 1)
            for i in range(1, 4):
                gated_attn(i)
            for i in range(4):
                full(dve, YC_USE + i)
                m = gates[:, i % 2, NB * (i // 2):NB * (i // 2) + NB]
                ga = gates[:, i % 2, D + NB * (i // 2):D + NB * (i // 2) + NB]
                v.tensor_tensor(m, m, bank(YC_USE + i)[:, :], ALU.mult).then_inc(bank_free[(YC_USE + i) % 4], 1)
                dve.wait_ge(bank_free[(YC_USE + i) % 4], (YC_USE + i) // 4 + 1)
                v.tensor_tensor(m, m, ga, ALU.add).then_inc(mixed, 1)
            dve.wait_ge(mod_ready, 16 * 16)
            dve.wait_ge(ebias_ready, 3 * PARTS)
            for i in range(4):
                tt, half = i // 2, i % 2
                cs = slice(NB * half, NB * half + NB)
                full(dve, WO_USE + i)
                use = WO_USE + i
                v.tensor_tensor(buf_k[:, 0, cs], bank(use)[:, :], modb[:, 0, cs], ALU.mult).then_inc(bank_free[use % 4], 1)
                dve.wait_ge(bank_free[use % 4], use // 4 + 1)
                v.tensor_tensor(x_tok[:, tt, cs], x_tok[:, tt, cs], buf_k[:, 0, cs], ALU.add).then_inc(x1_ready, 1)
            dve.wait_ge(in_norm2, 16)
            step(v.scalar_tensor_tensor(modb[:, 2, :], modb[:, 2, :], 1.0, norm2_b, ALU.add, ALU.mult))
            dve.wait_ge(x_ssq, 2 * (TT + 1))
            step(v.reciprocal(rstd[:, 0:TT], rstd[:, 0:TT]))
            for tt in range(TT):
                step(v.scalar_tensor_tensor(h2[:, tt, :], x_tok[:, tt, :], rstd[:, tt:tt + 1], modb[:, 2, :],
                                            ALU.mult, ALU.mult))
                v.tensor_tensor(h2[:, tt, :], h2[:, tt, :], modb[:, 1, :], ALU.add).then_inc(h2_ready, 1)
            v.memset(zero_b, 0.0).then_inc(h2_ready, 1)
            full(dve, LG_USE)
            use = LG_USE
            v.tensor_tensor(lg, bank(use)[:, 0:TT * EXPERTS].rearrange("p (t e) -> p t e", t=TT),
                            br_b[:].unsqueeze(1).to_broadcast([P, TT, EXPERTS]), ALU.add).then_inc(bank_free[use % 4], 1)
            dve.wait_ge(bank_free[use % 4], use // 4 + 1)
            for tt in range(TT):
                step(v.max(top[:, tt, :], lg[:, tt, :]))
                step(v.max_index(topi[:, tt, :], top[:, tt, :], lg[:, tt, :]))
                ins = v.tensor_scalar(topf[:, tt, 0:TOPK], top[:, tt, 0:TOPK], top[:, tt, 0:1], None, ALU.subtract)
                if tt == 0:
                    step(ins)
                else:
                    ins.then_inc(lg_ready, 1)
            dve.wait_ge(tw_ready, TT)
            step(v.tensor_copy(topf[:, :, 4:8], topi[:, :, 0:TOPK]))
            for tt in range(TT):
                step(v.reciprocal(tw[:, tt, 5:6], tw[:, tt, 4:5]))
                step(v.tensor_scalar(tw[:, tt, 0:TOPK], tw[:, tt, 0:TOPK], tw[:, tt, 5:6], None, ALU.mult))
                step(v.tensor_scalar(comb[:, tt, :], iota_e[:, 0:EXPERTS], topf[:, tt, 4:5], tw[:, tt, 0:1],
                                     ALU.is_equal, ALU.mult))
                for k in range(1, TOPK):
                    step(v.tensor_scalar(comb4[:, tt, :], iota_e[:, 0:EXPERTS], topf[:, tt, 4 + k:5 + k],
                                         tw[:, tt, k:k + 1], ALU.is_equal, ALU.mult))
                    step(v.tensor_tensor(comb[:, tt, :], comb[:, tt, :], comb4[:, tt, :], ALU.add))
            v.tensor_scalar(routed[:], comb[:], 0.0, None, ALU.is_gt).then_inc(routed_ready, 1)
            full(dve, RT_USE)
            full(dve, CNT_USE)
            step(v.tensor_copy(combT[:], bank(RT_USE)[0:EXPERTS, 0:T]))
            v.tensor_copy(routedT[:], bank(RT_USE)[0:EXPERTS, T:2 * T]).then_inc(bank_free[RT_USE % 4], 1)
            dve.wait_ge(bank_free[RT_USE % 4], RT_USE // 4 + 1)
            step(v.scalar_tensor_tensor(rankT[:], bank(CNT_USE)[0:EXPERTS, 0:T], -UNROUTED, routedT[:], ALU.add, ALU.mult))
            step(v.tensor_scalar(rankT[:], rankT[:], UNROUTED, None, ALU.add))
            v.tensor_copy(ecol[0:EXPERTS, 0:1], bank(CNT_USE)[0:EXPERTS, T:T + 1]).then_inc(bank_free[CNT_USE % 4], 1)
            dve.wait_ge(bank_free[CNT_USE % 4], CNT_USE // 4 + 1)
            e = slice(0, EXPERTS)
            step(v.tensor_scalar(ecol[e, 1:2], ecol[e, 0:1], 0.0, None, ALU.is_gt))
            step(v.tensor_tensor(ecol[e, 1:2], ecol[e, 1:2], first[:], ALU.max))
            step(v.tensor_copy(ecol[e, 2:3], ecol[e, 1:2]))
            for k in range(1, T // SLOTS):
                ins = v.scalar_tensor_tensor(ecol[e, 1:2], ecol[e, 0:1], float(SLOTS * k), ecol[e, 1:2], ALU.is_gt, ALU.add)
                if k < T // SLOTS - 1:
                    step(ins)
                else:
                    ins.then_inc(m_ready, 1)
            full(dve, END_USE)
            v.tensor_copy(ecol[:, 3:6], bank(END_USE)[0:3 * EXPERTS, 0:3]).then_inc(bank_free[END_USE % 4], 1)
            dve.wait_ge(bank_free[END_USE % 4], END_USE // 4 + 1)
            step(v.tensor_scalar(u_end, iota_e[0:3 * EXPERTS, :], ecol[:, 3:4], None, ALU.is_ge))
            step(v.scalar_tensor_tensor(onehot[:], iota_e[0:3 * EXPERTS, :], ecol[:, 5:6], u_end, ALU.is_ge, ALU.subtract))
            step(v.tensor_scalar(ubase, iota_e[e, :], ecol[e, 5:6], -float(SLOTS), ALU.subtract, ALU.mult))
            step(v.tensor_tensor(ubase, ubase, onehot[e, :], ALU.mult))
            step(v.tensor_tensor(ecol[e, 6:7], ecol[e, 4:5], ecol[e, 2:3], ALU.subtract))
            step(v.tensor_scalar(ecol[e, 8:9], ecol[e, 5:6], -1.0, 0.0, ALU.add, ALU.max))
            step(v.tensor_scalar(l_end, iota_e[e, :], ecol[e, 4:5], None, ALU.is_ge))
            step(v.scalar_tensor_tensor(l_one, iota_e[e, :], ecol[e, 6:7], l_end, ALU.is_ge, ALU.subtract))
            v.tensor_scalar(ecol[e, 7:8], ecol[e, 4:5], 16.0, None, ALU.mult).then_inc(oh_ready, 1)
            full(dve, UN_USE)
            b = bank(UN_USE)
            v.tensor_copy(unit_i[:], b[0:1, 256:256 + 3 * UCOLS + 2]).then_inc(units_ready, 1)
            step(v.tensor_copy(upos, b[:, 0:TT * UCOLS].rearrange("p (t u) -> p t u", t=TT)))
            v.tensor_copy(uwt, b[:, 128:128 + TT * UCOLS].rearrange("p (t u) -> p t u", t=TT)).then_inc(units_ready, 1)
            dve.wait_ge(units_ready, 2)
            count = dve.value_load(unit_i[0:1, 3 * UCOLS:3 * UCOLS + 1], min_val=TOPK, max_val=47)

            def make_pick(u):
                for tt in range(TT):
                    ins = v.tensor_scalar(pick[:, tt, :], iota_s[:, 0, :], upos[:, tt, bass.ds(u, 1)], None, ALU.is_equal)
                ins.then_inc(pick_ready, 1)

            def make_sel(u):
                v.tensor_copy(sel, onehot[:, bass.ds(u, 1)].to_broadcast([3 * EXPERTS, SLOTS])).then_inc(sel_ready, 1)

            make_pick(0)
            make_sel(0)
            dve.wait_ge(h2_split, 4)
            v.memset(oe, 0.0).then_inc(oe_ready, 1)
            v.memset(Cmb, 0.0).then_inc(cmb_ready, 1)
            PER_UNIT = 4

            with dve.Fori(0, count) as u:
                def link(ins, k):
                    ins.then_inc(u_step, 1)
                    dve.wait_ge(u_step, u * PER_UNIT + k)

                dve.wait_ge(up_done[0], u + 1)
                for tt in range(TT):
                    ins = v.tensor_scalar(pickw[:, tt, :], iota_s[:].rearrange("p a s -> p (a s)"),
                                          upos[:, tt, bass.ds(u, 1)], uwt[:, tt, bass.ds(u, 1)],
                                          ALU.is_equal, ALU.mult)
                ins.then_inc(pickw_ready, 1)
                for a in range(2):
                    dve.wait_ge(up_done[a], u + 1)
                    pairs = UP[a][:, :].rearrange("p (f two) -> p f two", two=2)
                    v.tensor_scalar(glu, pairs[:, :, 0], LIMIT, None, ALU.min).then_inc(glu_ready[a], 1)
                    link(v.tensor_scalar(lin, pairs[:, :, 1], LIMIT, -LIMIT, ALU.min, ALU.max), 2 * a + 1)
                    dve.wait_ge(glu_ready[a], u + 1)
                    link(v.scalar_tensor_tensor(gl, lin, 1.0, glu, ALU.add, ALU.mult), 2 * a + 2)
                    dve.wait_ge(sg_ready[a], u + 1)
                    v.tensor_tensor(act[:, a, :], gl, sg, ALU.mult).then_inc(act_ready[a], 1)
                    if a == 0:
                        dve.wait_ge(gathered, u + 1)
                        make_pick(u + 1)
                dve.wait_ge(t_done[1], u + 1)
                make_sel(u + 1)
            dve.wait_ge(combined, count + 1)
            for tt in range(TT):
                for i in range(2):
                    cs = slice(NB * i, NB * i + NB)
                    k = 2 * tt + i
                    v.tensor_tensor(buf_k[:, tt, cs], Y[tt][i][:, :], modb[:, 3, cs], ALU.mult).then_inc(y_gated, 1)
                    dve.wait_ge(y_gated, k + 1)
                    v.tensor_tensor(x_tok[:, tt, cs], x_tok[:, tt, cs], buf_k[:, tt, cs], ALU.add).then_inc(out_ready, 1)

        @block.tensor
        def _(pe):
            t = nc.tensor

            def wait_block(n):
                pe.wait_ge(blk_full[place(n)], 16 * loads_before[n])

            pe.wait_ge(c_ready, 1)
            for gi in range(4):
                wait_block(gi)
                for k in range(KD):
                    ins = t.matmul(PS[4][32 * gi:32 * gi + 32, :], c_act[:, k, :], blk(gi)[:, k, :],
                                   start=(k == 0), stop=(k == KD - 1))
                ins.then_inc(ada_done, 1)
            pe.wait_ge(made, MADE)
            pe.wait_ge(modrow_ready, 1)
            for gi in range(4):
                ins = t.matmul(PS[4 + gi][:, :], rowsel[:, gi, :], modrow, start=True, stop=True)
            ins.then_inc(bc_done, 1)
            for i in range(4):
                use = HT_USE + i
                fill(pe, use)
                tt = i // 2
                pe.wait_ge(h1_ready, i + 1)
                for k in range(4):
                    kk = 4 * (i % 2) + k
                    ins = t.transpose(bank(use)[:, P * k:P * k + P], h1[:, tt, P * kk:P * kk + P], ident[:])
                ins.then_inc(bank_full[use % 4], 1)
            pe.wait_ge(in_cols, 16 * 5)
            pe.wait_ge(h1_ready, 4)
            for k in range(KD):
                t.transpose(PS[4][:, TAPS * k:TAPS * k + TAPS], convw_rows[:, P * k:P * k + P], ident[0:TAPS, 0:TAPS])
            t.transpose(PS[5][:, 0:32], col_rows[:, :], ident[0:32, 0:32]).then_inc(colsT_done, 1)

            for i in range(4):
                pe.wait_ge(bank_free[(HT_USE + i) % 4], (HT_USE + i) // 4 + 1)
            for k in range(KD):
                use, n0 = CONV_USE + k, CONV0 + 2 * (k // 4)
                fill(pe, use)
                for half in range(2):
                    if k % 4 == 0:
                        wait_block(n0 + half)
                    for kk in range(KD):
                        ins = t.matmul(bank(use)[:, T * half:T * half + T], blk(n0 + half)[:, kk, P * (k % 4):P * (k % 4) + P],
                                       h1T[:, kk, :], start=(kk == 0), stop=(kk == KD - 1))
                ins.then_inc(bank_full[use % 4], 1)

            def proj(use, lhsT, tt, n, bias=None):
                fill(pe, use)
                if bias is not None:
                    t.matmul(bank(use)[:, :], bsel[:, bias, :], bias_b[:], start=True, stop=False)
                for k in range(KD):
                    ins = t.matmul(bank(use)[:, :], lhsT[:, k, P * tt:P * tt + P], blk(n)[:, k, :],
                                   start=(k == 0 and bias is None), stop=(k == KD - 1))
                ins.then_inc(bank_full[use % 4], 1)

            for i in range(8):
                if i % 2 == 0:
                    wait_block(QKV0 + i // 2)
                proj(QK_USE + i, h1T, i % 2, QKV0 + i // 2)
            for i in range(4):
                if i % 2 == 0:
                    wait_block(QKV0 + 4 + i // 2)
                proj(V_USE + i, h1T, i % 2, QKV0 + 4 + i // 2)

            for i in range(8):
                use = QKT_USE + i
                fill(pe, use)
                src = (q_tok, k_tok)[i // 4]
                col = 2 * (i % 4)
                pe.wait_ge(qk_ready, 16 if i >= 4 else 8)
                for hh in range(2):
                    for tt in range(TT):
                        ins = t.transpose(bank(use)[:, T * hh + P * tt:T * hh + P * tt + P],
                                          src[:, tt, P * (col + hh):P * (col + hh) + P], ident[:])
                ins.then_inc(bank_full[use % 4], 1)
            for gi in range(2):
                use = ADA_USE + gi
                fill(pe, use)
                for i in range(4):
                    n0 = ADA1 + 4 * gi + i
                    wait_block(n0)
                    for k in range(KD):
                        ins = t.matmul(bank(use)[32 * i:32 * i + 32, :], c_act[:, k, :], blk(n0)[:, k, :],
                                       start=(k == 0), stop=(k == KD - 1))
                    if i < 3:
                        ins.then_inc(ada_done, 1)
                    else:
                        ins.then_inc(bank_full[use % 4], 1)

            for i in range(8):
                if i >= 4:
                    pe.wait_ge(bank_free[(QKT_USE + i) % 4], (QKT_USE + i) // 4 + 1)

            def attend(h):
                use = aT_use(h)
                fill(pe, use)
                pe.wait_ge(pa_ready, h + 1)
                for k in range(3):
                    ins = t.transpose(bank(use)[:, P * k:P * k + P], pa[:, P * k:P * k + P], ident[:])
                ins.then_inc(bank_full[use % 4], 1)
                fill(pe, o_use(h))
                pe.wait_ge(bank_free[use % 4], use // 4 + 1)
                vh = v_tok[:, :, VD * h:VD * h + VD]
                use = o_use(h)
                o = bank(use)
                t.matmul(o[:, 0:VD], aT[:, 0:P], vh[:, 0, :], start=True, stop=True)
                t.matmul(o[:, VD:2 * VD], aT[:, P:2 * P], vh[:, 0, :], start=True, stop=False)
                t.matmul(o[:, VD:2 * VD], aT[:, 2 * P:3 * P], vh[:, 1, :], start=False, stop=True).then_inc(
                    bank_full[use % 4], 1)

            pe.wait_ge(bias_step, PARTS)
            for h in range(HEADS):
                par = h % 2
                if h >= 2:
                    pe.wait_ge(exp_done, 4 * (h - 1))
                for part in range(2):
                    sc = PS[4 + 2 * par + part]
                    rows = slice(HD * part, HD * part + HD)
                    t.matmul(sc[:, 0:384], identb[:], maskb[:], start=True, stop=False)
                    t.matmul(sc[:, 0:P], qT[rows, h, 0:P], kT[rows, h, 0:P], start=False, stop=False)
                    ins = t.matmul(sc[:, P:3 * P], qT[rows, h, P:2 * P], kT[rows, h, :], start=False, stop=True)
                ins.then_inc(sc_full, 1)
                if h % 2 == 0:
                    wait_block(GATE0 + h // 2)
                proj(gate_use(h), h1T, h % 2, GATE0 + h // 2, h // 2)
                if h:
                    attend(h - 1)
                if h == MEAN_AT:
                    fill(pe, MEAN_USE)
                    pe.wait_ge(conv_done, KD)
                    for k in range(KD):
                        ins = t.matmul(bank(MEAN_USE)[:, 0:T], ones[:], conv_acc[:, k, :], start=(k == 0), stop=(k == KD - 1))
                    ins.then_inc(bank_full[MEAN_USE % 4], 1)
                if h == VAR_AT:
                    fill(pe, VAR_USE)
                    pe.wait_ge(csq_ready, 1)
                    for k in range(KD):
                        ins = t.matmul(bank(VAR_USE)[:, 0:T], ones[:], u_conv[:, k, 0:T], start=(k == 0), stop=(k == KD - 1))
                    ins.then_inc(bank_full[VAR_USE % 4], 1)
            attend(HEADS - 1)
            pe.wait_ge(on_ready, 1)
            for i in range(4):
                use = OT_USE + i
                fill(pe, use)
                for k in range(4):
                    kk = 4 * (i % 2) + k
                    ins = t.transpose(bank(use)[:, P * k:P * k + P], o_tok[:, i // 2, P * kk:P * kk + P], ident[:])
                ins.then_inc(bank_full[use % 4], 1)
            for i in range(4):
                pe.wait_ge(bank_free[(OT_USE + i) % 4], (OT_USE + i) // 4 + 1)
            for i in range(4):
                if i % 2 == 0:
                    wait_block(AOUT0 + i // 2)
                proj(YA_USE + i, oT, i % 2, AOUT0 + i // 2)
            pe.wait_ge(swish_ready, KD)
            for i in range(4):
                if i % 2 == 0:
                    wait_block(COUT0 + i // 2)
                proj(YC_USE + i, conv_acc, i % 2, COUT0 + i // 2, 4 + i // 2)
            pe.wait_ge(mixed, 4)
            for i in range(4):
                use = MT_USE + i
                fill(pe, use)
                for k in range(4):
                    kk = 4 * (i % 2) + k
                    ins = t.transpose(bank(use)[:, P * k:P * k + P], gates[:, i // 2, P * kk:P * kk + P], ident[:])
                ins.then_inc(bank_full[use % 4], 1)
            for i in range(4):
                pe.wait_ge(bank_free[(MT_USE + i) % 4], (MT_USE + i) // 4 + 1)
            wait_block(WO0)
            wait_block(WO0 + 1)
            for i in range(4):
                use = WO_USE + i
                fill(pe, use)
                tt, n = i // 2, WO0 + i % 2
                for k in range(KD):
                    ins = t.matmul(bank(use)[:, :], mixT[:, k, P * tt:P * tt + P], blk(n)[:, k, :],
                                   start=(k == 0), stop=(k == KD - 1))
                ins.then_inc(bank_full[use % 4], 1)
            for i in range(4):
                use = H2T_USE + i
                fill(pe, use)
                pe.wait_ge(h2_ready, i // 2 + 1)
                for k in range(4):
                    kk = 4 * (i % 2) + k
                    ins = t.transpose(bank(use)[:, P * k:P * k + P], h2[:, i // 2, P * kk:P * kk + P], ident[:])
                ins.then_inc(bank_full[use % 4], 1)
            for i in range(4):
                pe.wait_ge(bank_free[(H2T_USE + i) % 4], (H2T_USE + i) // 4 + 1)
            pe.wait_ge(in_moe, 16)
            fill(pe, LG_USE)
            for tt in range(TT):
                for k in range(KD):
                    ins = t.matmul(bank(LG_USE)[:, EXPERTS * tt:EXPERTS * tt + EXPERTS], h2T[:, k, P * tt:P * tt + P],
                                   wr[:, k, :], start=(k == 0), stop=(k == KD - 1))
            ins.then_inc(bank_full[LG_USE % 4], 1)
            pe.wait_ge(routed_ready, 1)
            fill(pe, RT_USE)
            for j, src in enumerate((comb, routed)):
                for tt in range(TT):
                    ins = t.transpose(bank(RT_USE)[0:EXPERTS, T * j + P * tt:T * j + P * tt + P], src[:, tt, :], ident[:])
            ins.then_inc(bank_full[RT_USE % 4], 1)
            fill(pe, CNT_USE)
            for tt in range(TT):
                t.matmul(bank(CNT_USE)[0:EXPERTS, 0:T], routed[:, tt, :], upper[:, tt, :], start=(tt == 0), stop=(tt == TT - 1))
            for tt in range(TT):
                ins = t.matmul(bank(CNT_USE)[0:EXPERTS, T:T + 1], routed[:, tt, :], ones[:, 0:1], start=(tt == 0), stop=(tt == TT - 1))
            ins.then_inc(bank_full[CNT_USE % 4], 1)
            pe.wait_ge(m_ready, 1)
            fill(pe, END_USE)
            e = slice(0, EXPERTS)
            t.matmul(bank(END_USE)[0:3 * EXPERTS, 0:2], tri[:, 0, :, :].rearrange("p a b -> p (a b)"), ecol[e, 1:3],
                     start=True, stop=True)
            t.matmul(bank(END_USE)[0:3 * EXPERTS, 2:3], tri[:, 1, :, :].rearrange("p a b -> p (a b)"), ecol[e, 1:2],
                     start=True, stop=True).then_inc(bank_full[END_USE % 4], 1)
            pe.wait_ge(oh_ready, 1)
            fill(pe, UN_USE)
            b = bank(UN_USE)
            for tt in range(TT):
                ts = slice(P * tt, P * tt + P)
                t.matmul(b[:, UCOLS * tt:UCOLS * tt + UCOLS], rankT[:, ts], onehot[e, :], start=True, stop=False)
                t.matmul(b[:, UCOLS * tt:UCOLS * tt + UCOLS], ones[0:EXPERTS, :], ubase, start=False, stop=True)
            for tt in range(TT):
                t.matmul(b[:, P + UCOLS * tt:P + UCOLS * tt + UCOLS], combT[:, P * tt:P * tt + P], onehot[e, :], start=True, stop=True)
            for i, (col, rhs) in enumerate(((ecol[e, 7:8], onehot[e, :]), (ones[e, 0:1], l_end), (ecol[e, 8:9], l_one))):
                t.matmul(b[0:1, 256 + UCOLS * i:256 + UCOLS * i + UCOLS], col, rhs, start=True, stop=True)
            for i in range(2):
                ins = t.matmul(b[0:1, 256 + 3 * UCOLS + i:257 + 3 * UCOLS + i], ecol[e, 1 + i:2 + i], ones[e, 0:1],
                               start=True, stop=True)
            ins.then_inc(bank_full[UN_USE % 4], 1)
            pe.wait_ge(units_ready, 2)
            count = pe.value_load(unit_i[0:1, 3 * UCOLS:3 * UCOLS + 1], min_val=TOPK, max_val=47)

            def gather():
                for k in range(KD):
                    for tt in range(TT):
                        for i, part in enumerate(h2_parts):
                            ins = t.matmul(UP[0][:, SLOTS * k:SLOTS * k + SLOTS], part[:, tt, P * k:P * k + P],
                                           pick[:, tt, :], start=(tt == 0 and i == 0), stop=(tt == TT - 1 and i == 2))
                ins.then_inc(gathered, 1)

            def combine():
                for tt in range(TT):
                    for i in range(2):
                        rows = slice(SLOTS * i, SLOTS * i + SLOTS)
                        ins = t.matmul(Y[tt][i][:, :], Cmb[rows, P * tt:P * tt + P], oe[rows, :], start=False, stop=True,
                                       skip_group_check=True)
                ins.then_inc(combined, 1)

            pe.wait_ge(h2_ready, TT + 1)
            for tt in range(TT):
                for i in range(2):
                    t.matmul(Y[tt][i][:, :], zero_b[:, 0:P], zero_b[:, :], start=True, stop=True, skip_group_check=True)
            pe.wait_ge(pick_ready, 1)
            pe.wait_ge(h2_split, 4)
            gather()
            with pe.Fori(0, count) as u:
                landed = pe.value_load(unit_i[0:1, bass.ds(u, 1)], min_val=16, max_val=16 * EXPERTS)

                def bias(bank_, col):
                    for i in range(2):
                        t.matmul(bank_[SLOTS * i:SLOTS * i + SLOTS, :], sel, ebias[:, col + NB * i:col + NB * i + NB],
                                 start=True, stop=False)

                def up(a):
                    bias(UP[a], D * a)
                    for k in range(KD):
                        slot = 4 * a + k // 2
                        if k % 2 == 0:
                            pe.wait_ge(w_full[slot], landed)
                        for i in range(2):
                            ins = t.matmul(UP[a][SLOTS * i:SLOTS * i + SLOTS, :], xgT[:, k, :],
                                           wslot(slot)[:, k % 2, NB * i:NB * i + NB], start=False, stop=(k == KD - 1))
                        if k % 2 and k < KD - 1:
                            ins.then_inc(w_free, 1)
                    return ins

                def down(a):
                    if a == 0:
                        bias(DOWN, 2 * D)
                    for k in range(4):
                        slot = 8 + 2 * a + k // 2
                        if k % 2 == 0:
                            pe.wait_ge(w_full[slot], landed)
                        for i in range(2):
                            ins = t.matmul(DOWN[SLOTS * i:SLOTS * i + SLOTS, :],
                                           actT[:, a, k % 2, SLOTS * (k // 2):SLOTS * (k // 2) + SLOTS],
                                           wslot(slot)[:, k % 2, NB * i:NB * i + NB],
                                           start=False, stop=(a == 1 and k == 3))
                        if k == 1 or (k == 3 and a == 0):
                            ins.then_inc(w_free, 1)
                    return ins

                def transpose_act(a):
                    for j in range(2):
                        ins = t.transpose(TR[:, T * a + P * j:T * a + P * j + P], act[:, a, P * j:P * j + P], ident[:])
                    ins.then_inc(t_done[a], 1)

                pe.wait_ge(xg_ready, u + 1)
                pe.wait_ge(sel_ready, u + 1)
                up(0).then_inc(up_done[0], 1)
                up(1).then_inc(up_done[1], 1)
                pe.wait_ge(act_ready[0], u + 1)
                pe.wait_ge(cmb_ready, u + 1)
                transpose_act(0)
                pe.wait_ge(pick_ready, u + 2)
                gather()
                pe.wait_ge(oe_ready, u + 1)
                pe.wait_ge(actT_ready[0], u + 1)
                down(0)
                pe.wait_ge(act_ready[1], u + 1)
                transpose_act(1)
                combine()
                pe.wait_ge(pickw_ready, u + 1)
                pe.wait_ge(actT_ready[1], u + 1)
                for tt in range(TT):
                    ins = t.transpose(TR[:, P * tt:P * tt + P], pickw[:, tt, :], ident[:])
                ins.then_inc(ct_done, 1)
                down(1).then_inc(down_done, 1)
            pe.wait_ge(cmb_ready, count + 1)
            pe.wait_ge(oe_ready, count + 1)
            combine()


_INS = ['x', 'c', 'positions', 'w_ada', 'b_ada', 'norm1_g', 'w_in', 'conv_w', 'conv_b', 'conv_ln_g', 'conv_ln_b',
        'w_conv_out', 'b_conv_out', 'q_norm_g', 'k_norm_g', 'lambda_q1', 'lambda_k1', 'lambda_q2', 'lambda_k2',
        'subln_g', 'w_attn_out', 'b_gate', 'w_o', 'norm2_g', 'w_router', 'b_router', 'w_up', 'b_up', 'w_down', 'b_down']


def kernel(**inputs):
    import numpy as _np
    import concourse.bacc as _bacc
    from concourse.bass_utils import run_bass_kernel_spmd as _run

    nc = _bacc.Bacc("TRN2", target_bir_lowering=False, num_devices=1)
    arrays, args = {}, []
    for name in _INS:
        a = _np.ascontiguousarray(inputs[name])
        arrays[f"in_{name}"] = a
        args.append(nc.dram_tensor(f"in_{name}", a.shape, mybir.dt.from_np(a.dtype), kind="ExternalInput").ap())
    args.append(nc.dram_tensor("out_0", (1, T, D), F32, kind="ExternalOutput").ap())
    build(nc, *args)
    r = _run(nc, [arrays], core_ids=[0])
    return r.results[0]["out_0"]
```

```python
from contextlib import ExitStack

import concourse.bass as bass
from concourse import mybir

F32 = mybir.dt.float32
BF16 = mybir.dt.bfloat16
I32 = mybir.dt.int32
U32 = mybir.dt.uint32
ALU = mybir.AluOpType
ACT = mybir.ActivationFunctionType
AX = mybir.AxisListType.X

P = 128
T = 256
TT = T // P
D = 1024
KD = D // P
NB = 512
HEADS = 8
HD = 64
VD = 128
ROT = 16
HALF = ROT // 2
THETA = 500000.0
TAPS = 31
PAD = TAPS - 1
EXPERTS = 32
TOPK = 4
SLOTS = 64
UCOLS = 64
EPS = 1e-6
PARTS = 5
MEAN_AT, VAR_AT = 2, 4
ALPHA = 1.702
LIMIT = 7.0
LAM_INIT = 0.2
SUBLN = 1.0 - LAM_INIT
BLOCKF = KD * NB
RING = 6
NSLOT = 12
SLOTF = 2 * D
SPARE = 3
MASKED = -1e30
UNROUTED = -4096.0
TWO_PI = 6.283185307179586
TWO_PI_HI = 6.28125
TWO_PI_MID = 0.0019350051879882812
TWO_PI_LO = 3.0199159819567e-07
ROUND = 12582912.0
PI_F = 3.1415925


def build(nc, x, c, positions, w_ada, b_ada, norm1_g, w_in, conv_w, conv_b, conv_ln_g, conv_ln_b,
          w_conv_out, b_conv_out, q_norm_g, k_norm_g, lambda_q1, lambda_k1, lambda_q2, lambda_k2,
          subln_g, w_attn_out, b_gate, w_o, norm2_g, w_router, b_router, w_up, b_up, w_down, b_down, out):
    ctx = ExitStack()
    with ctx:
        def sb(name, shape, dt=F32):
            return ctx.enter_context(nc.sbuf_tensor(name, shape, dt))

        def sem(name):
            return ctx.enter_context(nc.semaphore(name))

        W = sb("weights", [P, RING * BLOCKF + SPARE * SLOTF])
        x_tok = sb("x_tok", [P, TT, D])
        buf_c = sb("buf_c", [P, TT, D])
        buf_d = sb("buf_d", [P, KD, T])
        u_conv = sb("u_conv", [P, KD, PAD + T])
        buf_k = sb("buf_k", [P, TT, D])
        qkT = sb("qkT", [P, 2, HEADS, T])
        v_tok = sb("v_tok", [P, TT, D])
        gates = W[:, RING * BLOCKF:RING * BLOCKF + 4 * D].rearrange("p (t n) -> p t n", t=TT)
        conv_acc = W[:, RING * BLOCKF + 4 * D:].rearrange("p (k t) -> p k t", k=KD)

        h1, q_tok = buf_c, buf_c
        oT = buf_c[:, :, :].rearrange("p a b -> p (a b)").rearrange("p (k t) -> p k t", k=KD)
        h1T, mixT = buf_d, buf_d
        k_tok, o_tok = buf_k, buf_k
        qT, kT = qkT[:, 0, :, :], qkT[:, 1, :, :]
        sg_conv = qkT[:, 0, 0:2, :]
        modb = qkT[:, :, :, :].rearrange("p a b c -> p (a b c)").rearrange("p (m d) -> p m d", m=4)
        flat_c = buf_c[:, :, :].rearrange("p a b -> p (a b)")
        pr = flat_c[:, 0:1536].rearrange("p (h c k) -> p h c k", h=2, c=2)
        pa = flat_c[:, 1536:1920]
        norm2_b = buf_c[:, 1, :]
        combT, rankT, routedT = (buf_k[0:EXPERTS, 1, T * i:T * i + T] for i in range(3))
        early = W[:, RING * BLOCKF:RING * BLOCKF + 4 * D]
        ada_bias = early[:, 0:3 * NB].rearrange("p (g n) -> p g n", g=3)
        g1_rows = early[:, 3 * NB:4 * NB]
        convw_rows = early[0:TAPS, 4 * NB:6 * NB]
        col_rows = early[0:32, 6 * NB:6 * NB + P]
        lam_in = early[:, 3200:3456].rearrange("p (i e) -> p i e", i=4)
        qk_g = early[:, 3456:3584].rearrange("p (i e) -> p i e", i=2)
        rot = early[:, 3584:3840].rearrange("p (i g j) -> p i g j", i=4, g=8)
        rope = early[:, 3840:3968].rearrange("p (i t j) -> p i t j", i=8, t=TT)
        qk_sq = early[:, 4 * NB:5 * NB]
        h2 = gates[:, 0, :].rearrange("p (t d) -> p t d", t=TT)
        h2T = gates[:, 1, :].rearrange("p (k t) -> p k t", k=KD)
        area_q = buf_d[:, :, :].rearrange("p a b -> p (a b)")
        area_k = u_conv[:, :, :].rearrange("p a b -> p (a b)")
        area_v = v_tok[:, :, :].rearrange("p a b -> p (a b)")
        xgT = area_q[:, 0:KD * SLOTS].rearrange("p (k s) -> p k s", k=KD)
        act = area_q[:, 512:1024].rearrange("p (a f) -> p a f", a=2)
        actT = area_q[:, 1024:1536].rearrange("p (a j s) -> p a j s", a=2, j=2)
        oe = area_q[:, 1536:2048]
        Cmb = area_k[:, 0:T]
        pick = area_k[:, 256:256 + TT * SLOTS // 2].bitcast(BF16).rearrange("p (t s) -> p t s", t=TT)
        pickw = area_k[:, 384:384 + TT * P].rearrange("p (t s) -> p t s", t=TT)
        sel = area_k[0:3 * EXPERTS, 640:640 + SLOTS // 2].bitcast(BF16)
        glu = area_k[:, 768:1024]
        lin = area_k[:, 1024:1280]
        sg = area_k[:, 1280:1536]
        gl = area_k[:, 1536:1792]
        ebias = area_v[0:3 * EXPERTS, 0:3 * D // 2].bitcast(BF16)
        ebias_f, ebias_r = buf_k[0:3 * EXPERTS, 0, :], buf_k[0:3 * EXPERTS, 1, :]
        h2_parts = [a.bitcast(BF16).rearrange("p (t d) -> p t d", t=TT) for a in (buf_c[:, 0, :], buf_c[:, 1, :], modb[:, 0, :])]
        h2_rest = (buf_k[:, 0, :], area_q[:, 0:D])
        wr = conv_acc[:, 4, :].rearrange("p (k e) -> p k e", k=KD)

        qk_junk = sb("qk_junk", [P, T])
        modrow2 = sb("modrow2", [P, 2, NB])
        modrow = modrow2[:, 0, :]
        bias_f = v_tok[0:96, 0, 0:NB]
        bias_b = sb("bias_b", [96, NB], BF16)
        bsel = sb("bsel", [96, 6, P], BF16)
        ln_std = sb("ln_std", [P, T])
        rowsel = sb("rowsel", [P, 4, P])
        ident = sb("ident", [P, P])
        identb = sb("identb", [P, P], BF16)
        gate2 = modb[:, 3, 0:NB]
        maskb = sb("maskb", [P, 3 * P], BF16)
        ones = sb("ones", [P, P])
        upper = sb("upper", [P, TT, T])
        cT = sb("cT", [P, KD])
        c_sig = sb("c_sig", [P, KD])
        c_act = sb("c_act", [P, KD, 32])
        convw = sb("convw", [P, KD, 32])
        cols = sb("cols", [P, 32])
        lam = sb("lam", [P, 8])
        pos_i = sb("pos_i", [P, TT], I32)
        pos_f = sb("pos_f", [P, TT])
        inv_f = sb("inv_f", [P, HALF])
        eps = sb("eps", [P, 1])
        ssq = sb("ssq", [P, 16])
        rstd = sb("rstd", [P, 16])
        qk_ss = sb("qk_ss", [P, 2, 8])
        aT = sb("aT", [P, 384])
        smax = sb("smax", [P, 2, 4])
        ssum = sb("ssum", [P, 2, 4])
        srec = sb("srec", [P, 4])
        br_b = sb("br_b", [P, EXPERTS])
        lg = area_k[:, 320:384].rearrange("p (t e) -> p t e", t=TT)
        top = sb("top", [P, TT, 8])
        topi = sb("topi", [P, TT, 8], U32)
        topf = sb("topf", [P, TT * TOPK])
        topn = sb("topn", [P, TT * TOPK])
        tw = sb("tw", [P, TT * TOPK])
        tsum = sb("tsum", [P, TT])
        comb = sb("comb", [P, TT, EXPERTS])
        comb4 = area_k[:, 768:1024].rearrange("p (k e) -> p k e", e=EXPERTS)
        routed = sb("routed", [P, TT, EXPERTS])
        iota_e = sb("iota_e", [P, UCOLS])
        iota_s = sb("iota_s", [P, 2, SLOTS])
        tri = sb("tri", [EXPERTS, 2, 3, EXPERTS])
        first = sb("first", [EXPERTS, 1])
        ecol = sb("ecol", [3 * EXPERTS, 10])
        onehot = sb("onehot", [3 * EXPERTS, UCOLS])
        ubase, l_end, l_one = (buf_k[0:EXPERTS, 1, 768 + UCOLS * i:768 + UCOLS * i + UCOLS] for i in range(3))
        u_end = buf_k[0:3 * EXPERTS, 1, 960:960 + UCOLS]
        unit_i = sb("unit_i", [1, 3 * UCOLS + 2], I32)
        unit_spare = sb("unit_spare", [1, UCOLS], I32)
        load_landed = sb("load_landed", [1, UCOLS], I32)
        load_spare = sb("load_spare", [1, UCOLS], I32)
        upos = area_k[:, 1792:1920].rearrange("p (t u) -> p t u", t=TT)
        uwt = area_k[:, 1920:2048].rearrange("p (t u) -> p t u", t=TT)

        PS = [ctx.enter_context(nc.psum_tensor(f"bank{i}", [P, NB], F32)) for i in range(8)]
        UP = [PS[0], PS[1]]
        DOWN, TR = PS[2], PS[3]
        Y = [[PS[4], PS[5]], [PS[6], PS[7]]]

        blk_full = [sem(f"blk_full{i}") for i in range(RING)]
        w_full = [sem(f"w_full{i}") for i in range(NSLOT)]
        w_free = sem("w_free")
        in_c, in_x, in_rows, in_cols, in_small, in_bias, in_norm2, in_moe, in_rowsb, in_eb, in_rows2 = (
            sem(n) for n in ("in_c", "in_x", "in_rows", "in_cols", "in_small", "in_bias", "in_norm2", "in_moe", "in_rowsb",
                             "in_eb", "in_rows2"))
        made = sem("constants_made")
        zeroed = sem("bias_rows_zeroed")
        c_ready, ada_done, modrow_ready, bc_done, h1_scaled = (
            sem(n) for n in ("c_ready", "ada_done", "modrow_ready", "bc_done", "h1_scaled"))
        h1_ready, colsT_done, cols_ready = (
            sem(n) for n in ("h1_ready", "colsT_done", "cols_ready"))
        bank_full = [sem(f"bank_full{i}") for i in range(4)]
        bank_free = [sem(f"bank_free{i}") for i in range(4)]
        glu_sig, qk_ready, rope_ready, rope_arg = (sem(n) for n in ("glu_sig", "qk_ready", "rope_ready", "rope_arg"))
        act_step, dve_step, x_ssq = sem("act_step"), sem("dve_step"), sem("x_ssq")
        sc_full, s_max, exp_done, pa_ready, o_ready = (
            sem(n) for n in ("sc_full", "s_max", "exp_done", "pa_ready", "o_ready"))
        on_ready, lam_arg = (
            sem(n) for n in ("on_ready", "lam_arg"))
        conv_done, csq_ready, ln_ready, sw_sig, swish_ready = (
            sem(n) for n in ("conv_done", "csq_ready", "ln_ready", "sw_sig", "swish_ready"))
        gate_ready, mixed, x1_ready, h2_ready = (
            sem(n) for n in ("gate_ready", "mixed", "x1_ready", "h2_ready"))
        lg_ready, tw_ready, routed_ready, comb_ready, m_ready, oh_ready, units_ready = (
            sem(n) for n in ("lg_ready", "tw_ready", "routed_ready", "comb_ready", "m_ready",
                             "oh_ready", "units_ready"))
        mod_ready, ebias_ready, h2_high, h2_split, bias_step, conv_sum = (
            sem(n) for n in ("mod_ready", "ebias_ready", "h2_high", "h2_split", "bias_step", "conv_sum"))
        pick_ready, pickw_ready, sel_ready, gathered, xg_ready = (
            sem(n) for n in ("pick_ready", "pickw_ready", "sel_ready", "gathered", "xg_ready"))
        up_done = [sem("up0_done"), sem("up1_done")]
        glu_ready = [sem("glu0_ready"), sem("glu1_ready")]
        sg_ready = [sem("sg0_ready"), sem("sg1_ready")]
        act_ready = [sem("act0_ready"), sem("act1_ready")]
        t_done = [sem("t0_done"), sem("t1_done")]
        actT_ready = [sem("actT0_ready"), sem("actT1_ready")]
        ct_done, cmb_ready, down_done, oe_ready, combined = (
            sem(n) for n in ("ct_done", "cmb_ready", "down_done", "oe_ready", "combined"))
        out_left, out_right, stored, u_step = sem("out_left"), sem("out_right"), sem("stored"), sem("u_step")

        def block_of(w, col):
            return w[0, :, col:col + NB].rearrange("(k p) n -> p k n", p=P)

        def ada_block(col):
            return w_ada[0, :, col:col + NB].rearrange("(p k) n -> p k n", k=KD)

        ADA_FIRST = (2, 3, 0, 1)
        blocks = [ada_block(NB * i) for i in ADA_FIRST]
        CONV0 = len(blocks)
        for i in (0, 2, 1, 3):
            blocks.append(block_of(w_in, NB * i))
        ADA0 = [len(blocks), 0]
        blocks += [ada_block(NB * i) for i in range(4, 8)]
        QK0 = len(blocks)
        blocks += [block_of(w_in, NB * i) for i in range(4, 8)]
        ADA0[1] = len(blocks)
        blocks += [ada_block(NB * i) for i in range(8, 12)]
        V0 = len(blocks)
        blocks += [block_of(w_in, NB * i) for i in range(8, 10)]
        GATE0 = len(blocks)
        blocks += [block_of(w_in, NB * i) for i in range(10, 14)]
        COUT0 = len(blocks)
        blocks += [block_of(w_conv_out, 0), block_of(w_conv_out, NB)]
        AOUT0 = len(blocks)
        blocks += [block_of(w_attn_out, 0), block_of(w_attn_out, NB)]
        WO0 = len(blocks)
        blocks += [block_of(w_o, 0), block_of(w_o, NB)]
        SHIFT = (RING - len(blocks)) % RING

        def place(n):
            return (n + SHIFT) % RING

        def blk(n):
            return W[:, place(n) * BLOCKF:(place(n) + 1) * BLOCKF].rearrange("p (k n) -> p k n", k=KD)

        loads_before = [sum(place(m) == place(n) for m in range(n + 1)) for n in range(len(blocks))]
        used = {}

        def used_by(n, use):
            used[n] = (bank_full[use % 4], use // 4 + 1)

        def wslot(i, spare=0):
            start = slice(i * SLOTF, (i + 1) * SLOTF)
            if i < SPARE:
                start = bass.ds(spare + i * SLOTF, SLOTF)
            return W[:, start].rearrange("p (k n) -> p k n", k=2)

        order = [("h1T", i) for i in range(4)] + [("conv", i) for i in range(8)]
        order += [("ada", 0)] + [("qk", i) for i in range(8)]
        order += [("ada", 1)] + [("v", i) for i in range(4)] + [("qkT", i) for i in range(8)]
        for h in range(HEADS + 1):
            if h < HEADS:
                order += [("gate", h)]
            if h:
                order += [("aT", h - 1), ("o", h - 1)]
            if h == MEAN_AT:
                order += [("mean", 0)]
            if h == VAR_AT:
                order += [("var", 0)]
        order += [("y_conv", i) for i in range(3)] + [("oT", i) for i in range(4)] + [("y_conv", 3)]
        order += [(name, i) for name in ("y_attn", "mixT", "w_o") for i in range(4)]
        order += [("h2T", 0), ("h2T", 1), ("logits", 0), ("h2T", 2), ("h2T", 3), ("logits", 1)]
        order += [(name, 0) for name in ("totals", "counts", "ends", "routing", "units")]
        use_of = {what: n for n, what in enumerate(order)}

        HT_USE = use_of["h1T", 0]
        CONV_USE = use_of["conv", 0]
        QK_USE = use_of["qk", 0]
        V_USE = use_of["v", 0]
        QKT_USE = use_of["qkT", 0]
        ADA_USE = [use_of["ada", 0], use_of["ada", 1]]
        YC_USE = [use_of["y_conv", i] for i in range(4)]
        OT_USE = use_of["oT", 0]
        YA_USE = use_of["y_attn", 0]
        MT_USE = use_of["mixT", 0]
        WO_USE = use_of["w_o", 0]
        H2T_USE = [use_of["h2T", i] for i in range(4)]
        LG_USE = [use_of["logits", i] for i in range(TT)]
        RT_USE = use_of["routing", 0]
        TOT_USE = use_of["totals", 0]
        CNT_USE = use_of["counts", 0]
        END_USE = use_of["ends", 0]
        UN_USE = use_of["units", 0]
        MEAN_USE, VAR_USE = use_of["mean", 0], use_of["var", 0]

        def gate_use(h):
            return use_of["gate", h]

        def aT_use(h):
            return use_of["aT", h]

        def o_use(h):
            return use_of["o", h]

        for i in range(4):
            used[i] = (ada_done, i + 1)
            used_by(CONV0 + i, CONV_USE + 3 + 4 * (i // 2))
            used_by(QK0 + i, QK_USE + 2 * i + 1)
            used_by(GATE0 + i, gate_use(2 * i + 1))
            for gi in range(2):
                used[ADA0[gi] + i] = (ada_done, 4 + 3 * gi + i + 1)
        for i in range(2):
            used_by(ADA0[i] + 3, ADA_USE[i])
            used_by(V0 + i, V_USE + 2 * i + 1)
            used_by(COUT0 + i, YC_USE[2 * i + 1])
            used_by(AOUT0 + i, YA_USE + 2 * i + 1)
            used_by(WO0 + i, WO_USE + 2 + i)

        def bank(use):
            return PS[use % 4]

        def full(eng, use):
            eng.wait_ge(bank_full[use % 4], use // 4 + 1)

        def fill(pe, use):
            if use >= 4:
                pe.wait_ge(bank_free[use % 4], use // 4)

        block = ctx.enter_context(nc.Block())

        @block.sync
        def _(sp):
            sp.dma_start(cT[:], c.rearrange("b (p k) -> p (b k)", k=KD)).then_inc(in_c, 16)
            sp.dma_start(ada_bias[:, 0, :],
                         b_ada[0:1, 0:4 * NB].rearrange("o (g n) -> g o n", g=4).to_broadcast([4, 32, NB])).then_inc(in_rows, 16)
            sp.dma_start(g1_rows[64:128, :],
                         norm1_g[0:1, :].rearrange("o (g n) -> g o n", g=2).to_broadcast([2, 32, NB])).then_inc(in_rows, 16)
            for n, src in enumerate(blocks):
                if n == 3:
                    sp.dma_start(x_tok[:], x[0].rearrange("(t p) d -> p t d", p=P)).then_inc(in_x, 16)
                if n >= RING:
                    sp.wait_ge(*used[n - RING])
                sp.dma_start(blk(n), src).then_inc(blk_full[place(n)], 16)

            def load_unit(e, wait, spare=0):
                for i in range(NSLOT):
                    wait(i)
                    pair = 2 * P * (i % 4)
                    if i < 8:
                        col = D * (i // 4)
                        src = w_up[0, e, pair:pair + 2 * P, col:col + D]
                    else:
                        src = w_down[0, e, pair:pair + 2 * P, :]
                    if not isinstance(e, int):
                        src = src.rearrange("o a n -> (o a) n")
                    sp.dma_start(wslot(i, spare), src.rearrange("(k p) n -> p k n", p=P)).then_inc(w_full[i], 16)

            load_unit(0, lambda i: sp.wait_ge(*used[len(blocks) - RING + i // 2]))
            sp.wait_ge(units_ready, 1)
            loads = sp.value_load(unit_i[0:1, 3 * UCOLS + 1:3 * UCOLS + 2], min_val=TOPK, max_val=EXPERTS)

            def slot_used(i, landed, before, before_last=None):
                if i < SPARE:
                    if before_last is not None:
                        sp.wait_ge(w_free, before_last * 9 + i + 1)
                    sp.wait_ge(w_full[i], landed)
                elif i % 4 == 3:
                    sp.wait_ge((up_done[0], up_done[1], down_done)[i // 4], before + 1)
                else:
                    sp.wait_ge(w_free, before * 9 + 3 * (i // 4) + i % 4 + 1)

            e1 = sp.value_load(unit_i[0:1, UCOLS + 1:UCOLS + 2], min_val=0, max_val=EXPERTS - 1)
            before1 = sp.value_load(unit_i[0:1, 2 * UCOLS + 1:2 * UCOLS + 2], min_val=0, max_val=46)
            sp.wait_ge(h2_high, TT)
            sp.wait_ge(h2_split, 3 * (TT - 1) + 1)
            load_unit(bass.ds(e1, 1), lambda i: slot_used(i, 16, before1), NSLOT * SLOTF)
            with sp.Fori(2, loads) as n:
                e = sp.value_load(unit_i[0:1, bass.ds(n + UCOLS, 1)], min_val=0, max_val=EXPERTS - 1)
                before = sp.value_load(unit_i[0:1, bass.ds(n + 2 * UCOLS, 1)], min_val=0, max_val=46)
                before_last = sp.value_load(unit_i[0:1, bass.ds(n + (2 * UCOLS - 1), 1)], min_val=0, max_val=46)
                spare = sp.value_load(load_spare[0:1, bass.ds(n, 1)], min_val=0, max_val=NSLOT * SLOTF)
                landed = sp.value_load(load_landed[0:1, bass.ds(n, 1)], min_val=16, max_val=16 * EXPERTS)
                load_unit(bass.ds(e, 1), lambda i: slot_used(i, landed, before, before_last), spare)
            for tt in range(TT):
                for i, part_ready in enumerate((out_left, out_right)):
                    cs = slice(NB * i, NB * i + NB)
                    sp.wait_ge(part_ready, tt + 1)
                    sp.dma_start(out[0, tt * P:(tt + 1) * P, cs], x_tok[:, tt, cs]).then_inc(stored, 16)
            sp.wait_ge(stored, 16 * 2 * TT)

        @block.gpsimd
        def _(pool):
            g = nc.gpsimd
            n = 0

            def step(ins):
                nonlocal n
                n += 1
                ins.then_inc(made, 1)
                pool.wait_ge(made, n)

            step(g.memset(ones[:], 1.0))
            step(g.memset(rowsel[:], 0.0))
            for gi in range(4):
                step(g.affine_select(out=rowsel[:, gi, :], in_=ones[:], pattern=[[0, P]], base=-32 * gi,
                                     channel_multiplier=1, compare_op=ALU.is_equal, fill=0.0))
            step(g.affine_select(out=ident[:], in_=ones[:], pattern=[[-1, P]], base=0, channel_multiplier=1,
                                 compare_op=ALU.is_equal, fill=0.0))
            step(g.tensor_copy(identb[:], ident[:]))
            step(g.memset(maskb[:], 0.0))
            for o in (0, 2 * P):
                step(g.affine_select(out=maskb[:, o:o + P], in_=maskb[:, o:o + P], pattern=[[-1, P]], base=0,
                                     channel_multiplier=1, compare_op=ALU.is_ge, fill=MASKED))
            step(g.memset(upper[:], 1.0))
            for tt in range(TT):
                step(g.affine_select(out=upper[:, tt, :], in_=upper[:, tt, :], pattern=[[1, T]], base=-P * tt,
                                     channel_multiplier=-1, compare_op=ALU.is_gt, fill=0.0))
            step(g.memset(tri[:], 1.0))
            for i, op in enumerate((ALU.is_ge, ALU.is_gt)):
                step(g.affine_select(out=tri[:, i, :, :], in_=tri[:, i, :, :], pattern=[[0, 3], [1, EXPERTS]], base=0,
                                     channel_multiplier=-1, compare_op=op, fill=0.0))
            step(g.memset(bsel[:], 1.0))
            for q in range(3):
                step(g.affine_select(out=bsel[32 * q:32 * q + 32, :, :], in_=bsel[32 * q:32 * q + 32, :, :],
                                     pattern=[[-1, 6], [0, P]], base=0, channel_multiplier=1,
                                     compare_op=ALU.is_equal, fill=0.0))
            step(g.affine_select(out=first[:], in_=ones[0:EXPERTS, 0:1], pattern=[[0, 1]], base=0,
                                 channel_multiplier=1, compare_op=ALU.is_equal, fill=0.0))
            step(g.iota(iota_e[:], pattern=[[1, UCOLS]], base=0, channel_multiplier=0,
                        allow_small_or_imprecise_dtypes=True))
            step(g.iota(iota_s[:], pattern=[[0, 2], [1, SLOTS]], base=0, channel_multiplier=0,
                        allow_small_or_imprecise_dtypes=True))
            for j in range(HALF):
                step(g.memset(inv_f[:, j:j + 1], float(THETA ** (-2.0 * j / ROT))))
            step(g.memset(u_conv[:, :, 0:PAD], 0.0))
            pool.wait_ge(in_rowsb, 16 * 6)
            m = 0

            def part(ins, sem_, n):
                ins.then_inc(sem_, 1)
                pool.wait_ge(sem_, n)

            def parts(dst, src, rest, sem_, n):
                part(g.tensor_copy(dst[0:96, :], src[0:96, :]), sem_, n + 1)
                part(g.tensor_tensor(rest[0:96, :], src[0:96, :], dst[0:96, :], ALU.subtract), sem_, n + 2)
                for q in (1, 2):
                    rows = slice(32 * q, 32 * q + 32)
                    part(g.tensor_copy(dst[rows, :], rest[rows, :]), sem_, n + 2 + q)
                part(g.tensor_tensor(dst[64:96, :], rest[64:96, :], dst[64:96, :], ALU.subtract), sem_, n + PARTS)

            parts(bias_b, bias_f, bias_f, bias_step, 0)
            for gi in range(2):
                pool.wait_ge(bank_free[ADA_USE[gi] % 4], ADA_USE[gi] // 4 + 1)
            pool.wait_ge(sc_full, HEADS)
            for gi in range(4):
                for q in range(4):
                    pool.dma_start(modb[32 * q:32 * q + 32, gi // 2:4:2, NB * (gi % 2):NB * (gi % 2) + NB],
                                   modrow2[32 * gi:32 * gi + 32, :, :]).then_inc(mod_ready, 16)
            for i in range(4):
                pool.wait_ge(bank_full[(OT_USE + i) % 4], (OT_USE + i) // 4 + 1)
            for piece in range(3):
                src = b_up[0, :, D * piece:D * piece + D] if piece < 2 else b_down[0]
                dst = ebias[:, D * piece:D * piece + D]
                for q in range(3):
                    pool.dma_start(ebias_f[32 * q:32 * q + 32, :], src).then_inc(in_eb, 16)
                pool.wait_ge(in_eb, 48 * (piece + 1))
                parts(dst, ebias_f, ebias_r, ebias_ready, PARTS * piece)
            for tt in range(TT):
                pool.wait_ge(h2_high, tt + 1)
                h2_tile, rest = h2[:, tt, :], h2_rest[tt]
                high, middle, low = (part_[:, tt, :] for part_ in h2_parts)
                part(g.tensor_tensor(rest, h2_tile, high, ALU.subtract), h2_split, 3 * tt + 1)
                part(g.tensor_copy(middle, rest), h2_split, 3 * tt + 2)
                if tt == 0:
                    pool.wait_ge(x1_ready, 2 * TT)
                part(g.tensor_tensor(low, rest, middle, ALU.subtract), h2_split, 3 * tt + 3)

        MADE = 1 + 1 + 4 + 1 + 1 + 1 + 2 + 1 + TT + (1 + 2) + (1 + 3) + 1 + 1 + 1 + HALF + 1

        @block.scalar
        def _(act_e):
            s = nc.scalar

            def load(dst, src, into):
                act_e.dma_start(dst, src).then_inc(into, 16)

            act_e.wait_ge(in_c, 16)
            s.activation(c_sig[:], cT[:], ACT.Sigmoid).then_inc(act_step, 1)
            act_e.wait_ge(zeroed, 1)
            load(convw_rows, conv_w[0], in_cols)
            for i, w in enumerate((conv_b, conv_ln_g, conv_ln_b)):
                load(col_rows[8 * i:8 * i + 8, :], w[0].rearrange("(k p) -> k p", p=P), in_cols)
            load(col_rows[24:25, :], subln_g, in_cols)
            for i, w in enumerate((lambda_q1, lambda_k1, lambda_q2, lambda_k2)):
                load(lam_in[:, i, :], w.to_broadcast([P, HD]), in_small)
            for i, w in enumerate((q_norm_g, k_norm_g)):
                load(qk_g[:, i, :], w.to_broadcast([P, HD]), in_small)
            for tt in range(TT):
                load(pos_i[:, tt:tt + 1], positions[0, tt * P:(tt + 1) * P].rearrange("(p o) -> p o", o=1), in_small)
            load(br_b[:], b_router.to_broadcast([P, EXPERTS]), in_bias)
            for q in range(3):
                load(bias_f[32 * q:32 * q + 4, :], b_gate[0].rearrange("(i n) -> i n", n=NB), in_rowsb)
                load(bias_f[32 * q + 4:32 * q + 6, :], b_conv_out[0].rearrange("(i n) -> i n", n=NB), in_rowsb)

            for gi in range(4):
                load(ada_bias[32 * gi:32 * gi + 32, 1:3, :],
                     b_ada[0:1, :].rearrange("o (g i n) -> o g i n", g=3, i=4)[:, 1:3, gi, :].to_broadcast([32, 2, NB]), in_rows2)
            act_e.wait_ge(in_x, 16)
            for tt in range(TT):
                s.activation(buf_k[:, tt, :], x_tok[:, tt, :], ACT.Square, accum_out=ssq[:, tt:tt + 1]).then_inc(x_ssq, 1)
            act_e.wait_ge(x_ssq, TT)
            act_e.wait_ge(zeroed, 1)
            s.activation(rstd[:, 0:TT], ssq[:, 0:TT], ACT.Sqrt, scale=1.0 / D, bias=eps[:]).then_inc(x_ssq, 1)
            for i in range(4):
                full(act_e, HT_USE + i)
                s.copy(h1T[:, 4 * (i // 2):4 * (i // 2) + 4, P * (i % 2):P * (i % 2) + P],
                       bank(HT_USE + i)[:, :].rearrange("p (k t) -> p k t", k=4)).then_inc(bank_free[(HT_USE + i) % 4], 1)
            act_e.wait_ge(rope_arg, 1)
            s.activation(rope[:, 6:8, :, :].rearrange("p a t j -> p (a t j)"),
                         rope[:, 4:6, :, :].rearrange("p a t j -> p (a t j)"), ACT.Sin).then_inc(rope_ready, 1)
            act_e.wait_ge(lam_arg, 1)
            s.activation(lam[:, 2:4], lam[:, 0:2], ACT.Exp).then_inc(lam_arg, 1)
            for k in range(KD):
                full(act_e, CONV_USE + k)
                if k >= 2:
                    act_e.wait_ge(bank_free[(CONV_USE + k - 2) % 4], (CONV_USE + k - 2) // 4 + 1)
                s.activation(sg_conv[:, k % 2, :], bank(CONV_USE + k)[:, T:2 * T], ACT.Sigmoid).then_inc(glu_sig, 1)
            for i in range(8):
                full(act_e, QK_USE + i)
                if i:
                    act_e.wait_ge(qk_ready, 2 * i - 1)
                s.activation(qk_sq, bank(QK_USE + i)[:, :], ACT.Square).then_inc(glu_sig, 1)
                act_e.wait_ge(qk_ready, 2 * i + 1)
                s.activation(qk_ss[:, 1, :], qk_ss[:, 0, :], ACT.Sqrt, scale=1.0 / HD, bias=eps[:]).then_inc(glu_sig, 1)
            act_e.wait_ge(bias_step, PARTS)
            for i in range(4):
                full(act_e, V_USE + i)
                s.copy(v_tok[:, i % 2, NB * (i // 2):NB * (i // 2) + NB], bank(V_USE + i)[:, :]).then_inc(
                    bank_free[(V_USE + i) % 4], 1)
            for i in range(8):
                full(act_e, QKT_USE + i)
                dst = (qT if i < 4 else kT)[:, 2 * (i % 4):2 * (i % 4) + 2, :]
                s.copy(dst, bank(QKT_USE + i)[:, :].rearrange("p (h t) -> p h t", h=2)).then_inc(
                    bank_free[(QKT_USE + i) % 4], 1)

            def attended(h):
                use = aT_use(h)
                full(act_e, use)
                s.copy(aT[:], bank(use)[:, 0:384]).then_inc(bank_free[use % 4], 1)
                use = o_use(h)
                full(act_e, use)
                for tt in range(TT):
                    s.activation(qk_junk[:, P * tt:P * tt + P], bank(use)[:, P * tt:P * tt + P], ACT.Square,
                                 accum_out=ssq[:, tt * 8 + h:tt * 8 + h + 1]).then_inc(o_ready, 1)

            for h in range(HEADS):
                par = h % 2
                act_e.wait_ge(s_max, h + 1)
                for part in range(2):
                    sc = PS[4 + 2 * par + part]
                    for blk_q, (a, b) in enumerate(((0, P), (P, 3 * P))):
                        at = 2 * blk_q + part
                        s.activation(pr[:, par, part, a:b], sc[:, a:b], ACT.Exp, scale=HD ** -0.5,
                                     bias=smax[:, par, at:at + 1], accum_out=ssum[:, par, at:at + 1]).then_inc(exp_done, 1)
                use = gate_use(h)
                full(act_e, use)
                s.copy(gates[:, h % 2, NB * (h // 2):NB * (h // 2) + NB], bank(use)[:, :]).then_inc(bank_free[use % 4], 1)
                if h:
                    attended(h - 1)
                if h == MEAN_AT + 1:
                    act_e.wait_ge(bank_free[MEAN_USE % 4], MEAN_USE // 4 + 1)
                    s.activation(u_conv[:, :, 0:T], conv_acc[:], ACT.Square).then_inc(csq_ready, 1)
                if h == VAR_AT:
                    full(act_e, VAR_USE)
                    s.activation(ln_std[:], bank(VAR_USE)[:, 0:T], ACT.Sqrt, scale=1.0 / D, bias=eps[:]).then_inc(
                        bank_free[VAR_USE % 4], 1)
                if h == VAR_AT + 1:
                    act_e.wait_ge(ln_ready, 1)
                    for k in range(KD):
                        s.activation(u_conv[:, k, 0:T], conv_acc[:, k, :], ACT.Sigmoid, scale=cols[:, 8 + k:9 + k],
                                     bias=cols[:, 16 + k:17 + k]).then_inc(sw_sig, 1)
            attended(HEADS - 1)
            act_e.wait_ge(o_ready, 2 * HEADS)
            s.activation(rstd[:], ssq[:], ACT.Sqrt, scale=1.0 / VD, bias=eps[:]).then_inc(o_ready, 1)
            for tt in range(TT):
                s.activation(gates[:, tt, :], gates[:, tt, :], ACT.Sigmoid).then_inc(gate_ready, 1)
            for i in range(4):
                full(act_e, OT_USE + i)
                s.activation(oT[:, 4 * (i % 2):4 * (i % 2) + 4, P * (i // 2):P * (i // 2) + P],
                             bank(OT_USE + i)[:, :].rearrange("p (k t) -> p k t", k=4), ACT.Copy,
                             scale=cols[:, 25:26]).then_inc(bank_free[(OT_USE + i) % 4], 1)
            for i in range(4):
                full(act_e, MT_USE + i)
                s.copy(mixT[:, 4 * (i % 2):4 * (i % 2) + 4, P * (i // 2):P * (i // 2) + P],
                       bank(MT_USE + i)[:, :].rearrange("p (k t) -> p k t", k=4)).then_inc(bank_free[(MT_USE + i) % 4], 1)
            load(wr, w_router[0].rearrange("(k p) e -> p k e", p=P), in_moe)
            load(norm2_b, norm2_g.to_broadcast([P, D]), in_norm2)
            for tt in range(TT):
                act_e.wait_ge(x1_ready, 2 * tt + 2)
                s.activation(gates[:, 0, D:2 * D], x_tok[:, tt, :], ACT.Square, accum_out=ssq[:, tt:tt + 1]).then_inc(x_ssq, 1)
                act_e.wait_ge(x_ssq, TT + 2 + 2 * tt)
                s.activation(rstd[:, tt:tt + 1], ssq[:, tt:tt + 1], ACT.Sqrt, scale=1.0 / D, bias=eps[:]).then_inc(x_ssq, 1)
                act_e.wait_ge(h2_ready, tt + 1)
                s.copy(h2_parts[0][:, tt, :], h2[:, tt, :]).then_inc(h2_high, 1)
                for i in (2 * tt, 2 * tt + 1):
                    use = H2T_USE[i]
                    full(act_e, use)
                    s.copy(h2T[:, 4 * (i % 2):4 * (i % 2) + 4, P * tt:P * tt + P],
                           bank(use)[:, :].rearrange("p (k t) -> p k t", k=4)).then_inc(bank_free[use % 4], 1)
            act_e.wait_ge(lg_ready, 1)
            s.activation(tw[:], topf[:], ACT.Exp).then_inc(tw_ready, 1)
            full(act_e, RT_USE)
            s.copy(routedT[:], bank(RT_USE)[0:EXPERTS, 0:T])
            s.copy(combT[:], bank(RT_USE)[0:EXPERTS, T:2 * T]).then_inc(bank_free[RT_USE % 4], 1)

            act_e.wait_ge(units_ready, 2)
            count = act_e.value_load(unit_i[0:1, 3 * UCOLS:3 * UCOLS + 1], min_val=TOPK, max_val=47)
            act_e.wait_ge(gathered, 1)
            s.copy(xgT, UP[0][:, :].rearrange("p (k s) -> p k s", k=KD)).then_inc(xg_ready, 1)
            with act_e.Fori(0, count) as u:
                def keep_act(a):
                    act_e.wait_ge(t_done[a], u + 1)
                    s.copy(actT[:, a, :, :], TR[:, T * a:T * a + T].rearrange("p (j s) -> p j s", j=2)).then_inc(
                        actT_ready[a], 1)

                act_e.wait_ge(glu_ready[0], u + 1)
                s.activation(sg, glu, ACT.Sigmoid, scale=ALPHA).then_inc(sg_ready[0], 1)
                keep_act(0)
                act_e.wait_ge(glu_ready[1], u + 1)
                s.activation(sg, glu, ACT.Sigmoid, scale=ALPHA).then_inc(sg_ready[1], 1)
                act_e.wait_ge(gathered, u + 2)
                s.copy(xgT, UP[0][:, :].rearrange("p (k s) -> p k s", k=KD)).then_inc(xg_ready, 1)
                keep_act(1)
                act_e.wait_ge(ct_done, u + 1)
                s.copy(Cmb, TR[:, 0:T]).then_inc(cmb_ready, 1)
            for tt in range(TT):
                act_e.wait_ge(combined, 2 * tt + 2)
                s.copy(x_tok[:, tt, NB:D], Y[tt][1][:, :]).then_inc(out_right, 1)

        @block.vector
        def _(dve):
            v = nc.vector
            n = 0

            def step(ins):
                nonlocal n
                n += 1
                ins.then_inc(dve_step, 1)
                dve.wait_ge(dve_step, n)

            step(v.memset(eps[:], EPS))
            step(v.memset(bias_f, 0.0))
            v.memset(col_rows, 0.0).then_inc(zeroed, 1)
            dve.wait_ge(act_step, 1)
            v.tensor_tensor(c_act[:], c_sig[:].unsqueeze(2).to_broadcast([P, KD, 32]),
                            cT[:].unsqueeze(2).to_broadcast([P, KD, 32]), ALU.mult).then_inc(c_ready, 1)
            dve.wait_ge(in_rows, 16 * 2)

            def first_row(n):
                gi = ADA_FIRST[n]
                rows = slice(32 * gi, 32 * gi + 32)
                dve.wait_ge(ada_done, n + 1)
                ins = v.tensor_tensor(modrow[rows, :], PS[n][rows, :], ada_bias[rows, 0, :], ALU.add)
                if gi >= 2:
                    step(ins)
                    ins = v.scalar_tensor_tensor(modrow[rows, :], modrow[rows, :], 1.0, g1_rows[rows, :], ALU.add, ALU.mult)
                ins.then_inc(modrow_ready, 1)

            for n_row in range(3):
                first_row(n_row)
            dve.wait_ge(x_ssq, TT + 1)
            step(v.reciprocal(rstd[:, 0:TT], rstd[:, 0:TT]))
            halves = [(tt, i) for i in range(2) for tt in range(TT)]
            for tt, i in halves:
                dve.wait_ge(bc_done, i + 1)
                v.scalar_tensor_tensor(h1[:, tt, NB * i:NB * i + NB], x_tok[:, tt, NB * i:NB * i + NB], rstd[:, tt:tt + 1],
                                       PS[6 + i][:, :], ALU.mult, ALU.mult).then_inc(h1_scaled, 1)
            first_row(3)
            for n_half, (tt, i) in enumerate(halves):
                hs = h1[:, tt, NB * i:NB * i + NB]
                dve.wait_ge(bc_done, i + 3)
                dve.wait_ge(h1_scaled, n_half + 1)
                v.tensor_tensor(hs, hs, PS[4 + i][:, :], ALU.add).then_inc(h1_ready, 1)
            dve.wait_ge(colsT_done, 1)
            step(v.tensor_copy(convw[:, :, 0:TAPS], PS[4][:, 0:KD * TAPS].rearrange("p (k w) -> p k w", k=KD)))
            step(v.tensor_copy(cols[:, 0:25], PS[5][:, 0:25]))
            v.tensor_scalar(cols[:, 25:26], cols[:, 24:25], SUBLN, None, ALU.mult).then_inc(cols_ready, 1)
            dve.wait_ge(cols_ready, 1)
            dve.wait_ge(in_small, 16 * 8)
            dve.wait_ge(made, MADE)
            step(v.tensor_copy(pos_f[:], pos_i[:]))
            ang = rope[:, 0, :, :]
            for tt in range(TT):
                step(v.tensor_scalar(rope[:, 0, tt, :], inv_f[:], pos_f[:, tt:tt + 1], None, ALU.mult))
            for k, (turn, add) in enumerate(((0.25, TWO_PI / 4), (0.0, 0.0))):
                r, t = rope[:, 4 + k, :, :], rope[:, 1, :, :]
                step(v.tensor_scalar(t, ang, 1.0 / TWO_PI, turn, ALU.mult, ALU.add))
                step(v.tensor_scalar(t, t, ROUND, None, ALU.add))
                step(v.tensor_scalar(t, t, -ROUND, None, ALU.add))
                step(v.scalar_tensor_tensor(r, t, -TWO_PI_HI, ang, ALU.mult, ALU.add))
                step(v.scalar_tensor_tensor(r, t, -TWO_PI_MID, r, ALU.mult, ALU.add))
                step(v.scalar_tensor_tensor(r, t, -TWO_PI_LO, r, ALU.mult, ALU.add))
                step(v.tensor_scalar(r, r, add, None, ALU.add))
                ins = v.tensor_scalar(r, r, PI_F, -PI_F, ALU.min, ALU.max)
                if k == 0:
                    step(ins)
                else:
                    ins.then_inc(rope_arg, 1)
            for i in range(2):
                step(v.tensor_tensor(lam_in[:, 2 * i, :], lam_in[:, 2 * i, :], lam_in[:, 2 * i + 1, :], ALU.mult))
                ins = v.tensor_reduce(lam[:, i:i + 1], lam_in[:, 2 * i, :], axis=AX, op=ALU.add)
                if i == 0:
                    step(ins)
                else:
                    ins.then_inc(lam_arg, 1)
            dve.wait_ge(lam_arg, 2)
            step(v.tensor_tensor(lam[:, 4:5], lam[:, 3:4], lam[:, 2:3], ALU.subtract))
            step(v.tensor_scalar(lam[:, 5:6], lam[:, 4:5], -LAM_INIT, None, ALU.add))

            def ada_row(gi):
                use = ADA_USE[gi]
                dve.wait_ge(in_rows2, 64)
                full(dve, use)
                v.tensor_tensor(modrow2[:, gi, :], bank(use)[:, :], ada_bias[:, 1 + gi, :], ALU.add).then_inc(bank_free[use % 4], 1)

            def glu_tile(k):
                use = CONV_USE + k
                dve.wait_ge(glu_sig, k + 1)
                v.tensor_tensor(u_conv[:, k, PAD:PAD + T], bank(use)[:, 0:T], sg_conv[:, k % 2, :],
                                ALU.mult).then_inc(bank_free[use % 4], 1)

            def conv(pair, w0, w1):
                nonlocal n
                tiles = (2 * pair, 2 * pair + 1)
                if w0 == 0:
                    for k in tiles:
                        dve.wait_ge(bank_free[(CONV_USE + k) % 4], (CONV_USE + k) // 4 + 1)
                for w in range(w0, w1):
                    for k in tiles:
                        acc = conv_acc[:, k, :]
                        if w == 0:
                            ins = v.tensor_scalar(acc, u_conv[:, k, 0:T], convw[:, k, 0:1], cols[:, k:k + 1], ALU.mult, ALU.add)
                        else:
                            dve.wait_ge(dve_step, n if w == w0 or (w == TAPS - 1 and k == tiles[1]) else n - 1)
                            ins = v.scalar_tensor_tensor(acc, u_conv[:, k, w:w + T], convw[:, k, w:w + 1], acc,
                                                         ALU.mult, ALU.add)
                        if w < TAPS - 1:
                            n += 1
                            ins.then_inc(dve_step, 1)
                        else:
                            ins.then_inc(conv_done, 1)

            glu_tile(0)
            glu_tile(1)
            conv(0, 0, 16)
            glu_tile(2)
            conv(0, 16, TAPS)
            glu_tile(3)
            glu_tile(4)
            conv(1, 0, 16)
            glu_tile(5)
            conv(1, 16, TAPS)
            glu_tile(6)
            glu_tile(7)
            ada_row(0)
            conv(2, 0, 16)
            dve.wait_ge(rope_ready, 1)
            for i in range(8):
                use = QK_USE + i
                tt, col, which = i % 2, NB * ((i // 2) % 2), i // 4
                dst = (q_tok, k_tok)[which][:, tt, col:col + NB].rearrange("p (g e) -> p g e", g=8)
                dve.wait_ge(glu_sig, KD + 2 * i + 1)
                v.tensor_reduce(qk_ss[:, 0, :], qk_sq.rearrange("p (g e) -> p g e", g=8), axis=AX,
                                op=ALU.add).then_inc(qk_ready, 1)
                dve.wait_ge(glu_sig, KD + 2 * i + 2)
                step(v.reciprocal(qk_ss[:, 1, :], qk_ss[:, 1, :]))
                if i == 0:
                    dve.wait_ge(bank_full[3], 1)
                v.tensor_tensor(dst, bank(use)[:, :].rearrange("p (g e) -> p g e", g=8),
                                qk_ss[:, 1, :].unsqueeze(2).to_broadcast([P, 8, HD]), ALU.mult).then_inc(bank_free[use % 4], 1)
                dve.wait_ge(bank_free[use % 4], use // 4 + 1)
                step(v.tensor_tensor(dst, dst, qk_g[:, which, :].unsqueeze(1).to_broadcast([P, 8, HD]), ALU.mult))
                cos = rope[:, 6, tt, :].unsqueeze(1).to_broadcast([P, 8, HALF])
                sin = rope[:, 7, tt, :].unsqueeze(1).to_broadcast([P, 8, HALF])
                x1, x2 = dst[:, :, 0:HALF], dst[:, :, HALF:ROT]
                v.tensor_tensor(rot[:, 0, :, :], x1, cos, ALU.mult)
                v.tensor_tensor(rot[:, 1, :, :], x2, sin, ALU.mult)
                v.tensor_tensor(rot[:, 2, :, :], x2, cos, ALU.mult)
                step(v.tensor_tensor(rot[:, 3, :, :], x1, sin, ALU.mult))
                v.tensor_tensor(x1, rot[:, 0, :, :], rot[:, 1, :, :], ALU.subtract)
                v.tensor_tensor(x2, rot[:, 2, :, :], rot[:, 3, :, :], ALU.add).then_inc(qk_ready, 1)
                if i == 0:
                    conv(2, 16, TAPS)
                if i >= 3:
                    conv(3, 4 * (i - 3), 4 * (i - 2))
            ada_row(1)

            def keep_o(h):
                use = o_use(h)
                if h == 0:
                    full(dve, QKT_USE + 7)
                dve.wait_ge(o_ready, 2 * h + 2)
                v.tensor_copy(o_tok[:, :, VD * h:VD * h + VD],
                              bank(use)[:, 0:2 * VD].rearrange("p (t e) -> p t e", t=2)).then_inc(bank_free[use % 4], 1)

            def swish(k):
                dve.wait_ge(sw_sig, k + 1)
                step(v.tensor_scalar(conv_acc[:, k, :], conv_acc[:, k, :], cols[:, 8 + k:9 + k], cols[:, 16 + k:17 + k],
                                     ALU.mult, ALU.add))
                v.tensor_tensor(conv_acc[:, k, :], conv_acc[:, k, :], u_conv[:, k, 0:T], ALU.mult).then_inc(swish_ready, 1)

            for h in range(HEADS):
                par = h % 2
                dve.wait_ge(sc_full, h + 1)
                for blk_q, (a, b) in enumerate(((0, P), (P, 3 * P))):
                    for part in range(2):
                        at = 2 * blk_q + part
                        ins = v.tensor_reduce(smax[:, par, at:at + 1], PS[4 + 2 * par + part][:, a:b], axis=AX, op=ALU.max)
                step(ins)
                v.tensor_scalar(smax[:, par, :], smax[:, par, :], -(HD ** -0.5), None, ALU.mult).then_inc(s_max, 1)
                if h < 2:
                    conv(3, (20, 26)[h], (26, TAPS)[h])
                dve.wait_ge(exp_done, 4 * h + 4)
                step(v.reciprocal(srec[:], ssum[:, par, :]))
                step(v.tensor_scalar(srec[:].rearrange("p (b c) -> p b c", c=2)[:, :, 1],
                                     srec[:].rearrange("p (b c) -> p b c", c=2)[:, :, 1], lam[:, 5:6], None, ALU.mult))
                if h:
                    full(dve, aT_use(h - 1))
                for blk_q, (a, b) in enumerate(((0, P), (P, 3 * P))):
                    step(v.tensor_scalar(pa[:, a:b], pr[:, par, 0, a:b], srec[:, 2 * blk_q:2 * blk_q + 1], None, ALU.mult))
                    ins = v.scalar_tensor_tensor(pa[:, a:b], pr[:, par, 1, a:b], srec[:, 2 * blk_q + 1:2 * blk_q + 2],
                                                 pa[:, a:b], ALU.mult, ALU.add)
                ins.then_inc(pa_ready, 1)
                if h:
                    keep_o(h - 1)
                if h == MEAN_AT:
                    full(dve, MEAN_USE)
                    v.scalar_tensor_tensor(conv_acc[:], bank(MEAN_USE)[:, 0:T].unsqueeze(1).to_broadcast([P, KD, T]),
                                           -1.0 / D, conv_acc[:], ALU.mult, ALU.add).then_inc(bank_free[MEAN_USE % 4], 1)
                if h == MEAN_AT - 1:
                    dve.wait_ge(conv_done, KD)
                    v.tensor_reduce(ln_std[:], conv_acc[:].rearrange("p k t -> p t k"), axis=AX,
                                    op=ALU.add).then_inc(conv_sum, 1)
                if h == VAR_AT - 1:
                    dve.wait_ge(csq_ready, 1)
                    v.tensor_reduce(ln_std[:], u_conv[:, :, 0:T].rearrange("p k t -> p t k"), axis=AX,
                                    op=ALU.add).then_inc(conv_sum, 1)
                if h == VAR_AT:
                    dve.wait_ge(bank_free[VAR_USE % 4], VAR_USE // 4 + 1)
                    step(v.reciprocal(ln_std[:], ln_std[:]))
                    v.tensor_tensor(conv_acc[:], conv_acc[:], ln_std[:].unsqueeze(1).to_broadcast([P, KD, T]),
                                    ALU.mult).then_inc(ln_ready, 1)
                if VAR_AT < h <= VAR_AT + 2:
                    for k in range(4):
                        swish(4 * (h - VAR_AT - 1) + k)
            keep_o(HEADS - 1)
            dve.wait_ge(o_ready, 2 * HEADS + 1)
            dve.wait_ge(bank_free[o_use(HEADS - 1) % 4], o_use(HEADS - 1) // 4 + 1)
            step(v.reciprocal(rstd[:], rstd[:]))
            v.tensor_tensor(o_tok[:].rearrange("p t (h e) -> p (t h) e", h=HEADS),
                            o_tok[:].rearrange("p t (h e) -> p (t h) e", h=HEADS),
                            rstd[:].unsqueeze(2).to_broadcast([P, 16, VD]), ALU.mult).then_inc(on_ready, 1)
            dve.wait_ge(gate_ready, TT)
            for i in range(4):
                full(dve, YC_USE[i])
                m = gates[:, i % 2, NB * (i // 2):NB * (i // 2) + NB]
                v.tensor_tensor(m, m, bank(YC_USE[i])[:, :], ALU.mult).then_inc(bank_free[YC_USE[i] % 4], 1)
            for i in range(4):
                use = YA_USE + i
                full(dve, use)
                m = gates[:, i % 2, NB * (i // 2):NB * (i // 2) + NB]
                ga = gates[:, i % 2, D + NB * (i // 2):D + NB * (i // 2) + NB]
                v.tensor_tensor(ga, ga, bank(use)[:, :], ALU.mult).then_inc(bank_free[use % 4], 1)
                dve.wait_ge(bank_free[use % 4], use // 4 + 1)
                v.tensor_tensor(m, m, ga, ALU.add).then_inc(mixed, 1)
            dve.wait_ge(mod_ready, 16 * 16)
            dve.wait_ge(in_norm2, 16)
            step(v.scalar_tensor_tensor(modb[:, 2, :], modb[:, 2, :], 1.0, norm2_b, ALU.add, ALU.mult))
            for tt in range(TT):
                for half in range(2):
                    cs = slice(NB * half, NB * half + NB)
                    use = WO_USE + 2 * tt + half
                    full(dve, use)
                    gated = conv_acc[:, 2 * half:2 * half + 2, :].rearrange("p a t -> p (a t)")
                    v.tensor_tensor(gated, bank(use)[:, :], modb[:, 0, cs], ALU.mult).then_inc(bank_free[use % 4], 1)
                    dve.wait_ge(bank_free[use % 4], use // 4 + 1)
                    v.tensor_tensor(x_tok[:, tt, cs], x_tok[:, tt, cs], gated, ALU.add).then_inc(x1_ready, 1)
                dve.wait_ge(x_ssq, TT + 3 + 2 * tt)
                step(v.reciprocal(rstd[:, tt:tt + 1], rstd[:, tt:tt + 1]))
                step(v.scalar_tensor_tensor(h2[:, tt, :], x_tok[:, tt, :], rstd[:, tt:tt + 1], modb[:, 2, :],
                                            ALU.mult, ALU.mult))
                v.tensor_tensor(h2[:, tt, :], h2[:, tt, :], modb[:, 1, :], ALU.add).then_inc(h2_ready, 1)
            step(v.tensor_copy(gate2[SLOTS:P, :], modb[SLOTS:P, 3, NB:D]))
            for tt in range(TT):
                use = LG_USE[tt]
                full(dve, use)
                v.tensor_tensor(lg[:, tt, :], bank(use)[:, 0:EXPERTS], br_b[:], ALU.add).then_inc(bank_free[use % 4], 1)
                dve.wait_ge(bank_free[use % 4], use // 4 + 1)
                step(v.max(top[:, tt, :], lg[:, tt, :]))
                step(v.max_index(topi[:, tt, :], top[:, tt, :], lg[:, tt, :]))
            v.tensor_tensor(topf[:].rearrange("p (t k) -> p t k", t=TT), top[:, :, 0:TOPK],
                            top[:, :, 0:1].to_broadcast([P, TT, TOPK]), ALU.subtract).then_inc(lg_ready, 1)
            step(v.tensor_copy(topn[:].rearrange("p (t k) -> p t k", t=TT), topi[:, :, 0:TOPK]))
            places = (P, TT * TOPK, EXPERTS)
            step(v.tensor_tensor(comb4, iota_e[:, 0:EXPERTS].unsqueeze(1).to_broadcast(places),
                                 topn[:].unsqueeze(2).to_broadcast(places), ALU.is_equal))
            v.tensor_reduce(routed[:], comb4.rearrange("p (t k) e -> p t e k", t=TT), axis=AX,
                            op=ALU.add).then_inc(routed_ready, 1)
            dve.wait_ge(ebias_ready, 3 * PARTS)
            dve.wait_ge(tw_ready, 1)
            by_tile = tw[:].rearrange("p (t k) -> p t k", t=TT)
            step(v.tensor_reduce(tsum[:], by_tile, axis=AX, op=ALU.add))
            step(v.reciprocal(tsum[:], tsum[:]))
            step(v.tensor_tensor(by_tile, by_tile, tsum[:].unsqueeze(2).to_broadcast([P, TT, TOPK]), ALU.mult))
            dve.wait_ge(routed_ready, 1)
            step(v.tensor_tensor(comb4, comb4, tw[:].unsqueeze(2).to_broadcast(places), ALU.mult))
            v.tensor_reduce(comb[:], comb4.rearrange("p (t k) e -> p t e k", t=TT), axis=AX,
                            op=ALU.add).then_inc(comb_ready, 1)
            full(dve, TOT_USE)
            v.tensor_copy(ecol[0:EXPERTS, 0:1], bank(TOT_USE)[0:EXPERTS, 0:1]).then_inc(bank_free[TOT_USE % 4], 1)
            dve.wait_ge(bank_free[TOT_USE % 4], TOT_USE // 4 + 1)
            e = slice(0, EXPERTS)
            step(v.tensor_scalar(ecol[e, 1:2], ecol[e, 0:1], 0.0, None, ALU.is_gt))
            step(v.tensor_tensor(ecol[e, 1:2], ecol[e, 1:2], first[:], ALU.max))
            step(v.tensor_copy(ecol[e, 2:3], ecol[e, 1:2]))
            for k in range(1, T // SLOTS):
                ins = v.scalar_tensor_tensor(ecol[e, 1:2], ecol[e, 0:1], float(SLOTS * k), ecol[e, 1:2], ALU.is_gt, ALU.add)
                if k < T // SLOTS - 1:
                    step(ins)
                else:
                    ins.then_inc(m_ready, 1)
            full(dve, END_USE)
            v.tensor_copy(ecol[:, 3:6], bank(END_USE)[0:3 * EXPERTS, 0:3]).then_inc(bank_free[END_USE % 4], 1)
            dve.wait_ge(bank_free[END_USE % 4], END_USE // 4 + 1)
            step(v.tensor_scalar(u_end, iota_e[0:3 * EXPERTS, :], ecol[:, 3:4], None, ALU.is_ge))
            step(v.scalar_tensor_tensor(onehot[:], iota_e[0:3 * EXPERTS, :], ecol[:, 5:6], u_end, ALU.is_ge, ALU.subtract))
            step(v.tensor_scalar(ubase, iota_e[e, :], ecol[e, 5:6], -float(SLOTS), ALU.subtract, ALU.mult))
            v.tensor_tensor(ubase, ubase, onehot[e, :], ALU.mult).then_inc(oh_ready, 1)
            step(v.tensor_tensor(ecol[e, 6:7], ecol[e, 4:5], ecol[e, 2:3], ALU.subtract))
            step(v.tensor_scalar(ecol[e, 8:9], ecol[e, 5:6], -1.0, 0.0, ALU.add, ALU.max))
            step(v.tensor_scalar(l_end, iota_e[e, :], ecol[e, 4:5], None, ALU.is_ge))
            step(v.scalar_tensor_tensor(l_one, iota_e[e, :], ecol[e, 6:7], l_end, ALU.is_ge, ALU.subtract))
            step(v.tensor_scalar(ecol[e, 7:8], ecol[e, 4:5], 16.0, None, ALU.mult))
            full(dve, CNT_USE)
            dve.wait_ge(bank_free[RT_USE % 4], RT_USE // 4 + 1)
            v.scalar_tensor_tensor(rankT[:], bank(CNT_USE)[0:EXPERTS, 0:T], -UNROUTED, routedT[:], ALU.add,
                                   ALU.mult).then_inc(bank_free[CNT_USE % 4], 1)
            dve.wait_ge(bank_free[CNT_USE % 4], CNT_USE // 4 + 1)
            v.tensor_scalar(rankT[:], rankT[:], UNROUTED, None, ALU.add).then_inc(oh_ready, 1)
            step(v.tensor_scalar(load_landed[:], iota_e[0:1, :], 16.0, None, ALU.mult))
            step(v.tensor_copy(load_spare[:], iota_e[0:1, :]))
            step(v.tensor_scalar(load_spare[:], load_spare[:], 1, None, ALU.bitwise_and))
            step(v.tensor_scalar(load_spare[:], load_spare[:], float(NSLOT * SLOTF), None, ALU.mult))
            full(dve, UN_USE)
            b = bank(UN_USE)
            v.tensor_copy(unit_i[:], b[0:1, 256:256 + 3 * UCOLS + 2]).then_inc(units_ready, 1)
            dve.wait_ge(units_ready, 1)
            step(v.tensor_scalar(unit_spare[:], unit_i[:, 0:UCOLS], 16, 16, ALU.bitwise_and, ALU.bitwise_xor))
            step(v.tensor_copy(upos, b[:, 0:TT * UCOLS].rearrange("p (t u) -> p t u", t=TT)))
            v.tensor_copy(uwt, b[:, 128:128 + TT * UCOLS].rearrange("p (t u) -> p t u", t=TT)).then_inc(units_ready, 1)
            dve.wait_ge(units_ready, 2)

            def make_pick(u):
                for tt in range(TT):
                    ins = v.tensor_scalar(pick[:, tt, :], iota_s[:, 0, :], upos[:, tt, bass.ds(u, 1)], None, ALU.is_equal)
                ins.then_inc(pick_ready, 1)

            def make_sel(u):
                v.tensor_copy(sel, onehot[:, bass.ds(u, 1)].to_broadcast([3 * EXPERTS, SLOTS])).then_inc(sel_ready, 1)

            make_pick(0)
            make_sel(0)
            count = dve.value_load(unit_i[0:1, 3 * UCOLS:3 * UCOLS + 1], min_val=TOPK, max_val=47)

            dve.wait_ge(h2_split, 3 * TT)
            v.memset(oe, 0.0).then_inc(oe_ready, 1)
            v.memset(Cmb, 0.0).then_inc(cmb_ready, 1)
            PER_UNIT = 4

            with dve.Fori(0, count) as u:
                def link(ins, k):
                    ins.then_inc(u_step, 1)
                    dve.wait_ge(u_step, u * PER_UNIT + k)

                dve.wait_ge(up_done[0], u + 1)
                for tt in range(TT):
                    ins = v.tensor_scalar(pickw[:, tt, :], iota_s[:].rearrange("p a s -> p (a s)"),
                                          upos[:, tt, bass.ds(u, 1)], uwt[:, tt, bass.ds(u, 1)],
                                          ALU.is_equal, ALU.mult)
                ins.then_inc(pickw_ready, 1)
                for a in range(2):
                    dve.wait_ge(up_done[a], u + 1)
                    pairs = UP[a][:, :].rearrange("p (f two) -> p f two", two=2)
                    v.tensor_scalar(glu, pairs[:, :, 0], LIMIT, None, ALU.min).then_inc(glu_ready[a], 1)
                    link(v.tensor_scalar(lin, pairs[:, :, 1], LIMIT, -LIMIT, ALU.min, ALU.max), 2 * a + 1)
                    dve.wait_ge(glu_ready[a], u + 1)
                    link(v.scalar_tensor_tensor(gl, lin, 1.0, glu, ALU.add, ALU.mult), 2 * a + 2)
                    dve.wait_ge(sg_ready[a], u + 1)
                    v.tensor_tensor(act[:, a, :], gl, sg, ALU.mult).then_inc(act_ready[a], 1)
                    if a == 0:
                        dve.wait_ge(gathered, u + 1)
                        make_pick(u + 1)
                dve.wait_ge(t_done[1], u + 1)
                make_sel(u + 1)
                dve.wait_ge(down_done, u + 1)
                v.tensor_tensor(oe, DOWN[:, :], gate2, ALU.mult).then_inc(oe_ready, 1)
            for tt in range(TT):
                dve.wait_ge(combined, 2 * tt + 1)
                v.tensor_copy(x_tok[:, tt, 0:NB], Y[tt][0][:, :]).then_inc(out_left, 1)

        @block.tensor
        def _(pe):
            t = nc.tensor

            def wait_block(n):
                pe.wait_ge(blk_full[place(n)], 16 * loads_before[n])

            pe.wait_ge(c_ready, 1)
            for n, gi in enumerate(ADA_FIRST):
                rows = slice(32 * gi, 32 * gi + 32)
                wait_block(n)
                for k in range(KD):
                    ins = t.matmul(PS[n][rows, :], c_act[:, k, :], blk(n)[:, k, :], start=(k == 0), stop=(k == KD - 1))
                ins.then_inc(ada_done, 1)
                if n == 0:
                    pe.wait_ge(made, MADE)
                pe.wait_ge(modrow_ready, n + 1)
                t.matmul(PS[4 + gi][:, :], rowsel[rows, gi, :], modrow[rows, :], start=True, stop=True).then_inc(bc_done, 1)
            for i in range(4):
                use = HT_USE + i
                fill(pe, use)
                tt = i % 2
                pe.wait_ge(h1_ready, i + 1)
                for k in range(4):
                    kk = 4 * (i // 2) + k
                    ins = t.transpose(bank(use)[:, P * k:P * k + P], h1[:, tt, P * kk:P * kk + P], ident[:])
                ins.then_inc(bank_full[use % 4], 1)
            pe.wait_ge(in_cols, 16 * 5)
            pe.wait_ge(h1_ready, 4)
            for k in range(KD):
                t.transpose(PS[4][:, TAPS * k:TAPS * k + TAPS], convw_rows[:, P * k:P * k + P], ident[0:TAPS, 0:TAPS])
            t.transpose(PS[5][:, 0:32], col_rows[:, :], ident[0:32, 0:32]).then_inc(colsT_done, 1)

            for i in range(4):
                pe.wait_ge(bank_free[(HT_USE + i) % 4], (HT_USE + i) // 4 + 1)
            for k in range(KD):
                use, n0 = CONV_USE + k, CONV0 + 2 * (k // 4)
                fill(pe, use)
                for half in range(2):
                    if k % 4 == 0:
                        wait_block(n0 + half)
                    for kk in range(KD):
                        ins = t.matmul(bank(use)[:, T * half:T * half + T], blk(n0 + half)[:, kk, P * (k % 4):P * (k % 4) + P],
                                       h1T[:, kk, :], start=(kk == 0), stop=(kk == KD - 1))
                ins.then_inc(bank_full[use % 4], 1)

            def proj(use, lhsT, tt, n, bias=None):
                fill(pe, use)
                if bias is not None:
                    t.matmul(bank(use)[:, :], bsel[:, bias, :], bias_b[:], start=True, stop=False)
                for k in range(KD):
                    ins = t.matmul(bank(use)[:, :], lhsT[:, k, P * tt:P * tt + P], blk(n)[:, k, :],
                                   start=(k == 0 and bias is None), stop=(k == KD - 1))
                ins.then_inc(bank_full[use % 4], 1)

            def ada_rows(gi):
                use = ADA_USE[gi]
                fill(pe, use)
                for i in range(4):
                    wait_block(ADA0[gi] + i)
                for i in range(4):
                    for k in range(KD):
                        ins = t.matmul(bank(use)[32 * i:32 * i + 32, :], c_act[:, k, :], blk(ADA0[gi] + i)[:, k, :],
                                       start=(k == 0), stop=(k == KD - 1))
                    ins.then_inc(*((ada_done, 1) if i < 3 else (bank_full[use % 4], 1)))

            ada_rows(0)
            for i in range(8):
                if i % 2 == 0:
                    wait_block(QK0 + i // 2)
                proj(QK_USE + i, h1T, i % 2, QK0 + i // 2)
            ada_rows(1)
            for i in range(4):
                if i % 2 == 0:
                    wait_block(V0 + i // 2)
                proj(V_USE + i, h1T, i % 2, V0 + i // 2)

            for i in range(8):
                use = QKT_USE + i
                fill(pe, use)
                src = (q_tok, k_tok)[i // 4]
                col = 2 * (i % 4)
                pe.wait_ge(qk_ready, 16 if i >= 4 else 8)
                for hh in range(2):
                    for tt in range(TT):
                        ins = t.transpose(bank(use)[:, T * hh + P * tt:T * hh + P * tt + P],
                                          src[:, tt, P * (col + hh):P * (col + hh) + P], ident[:])
                ins.then_inc(bank_full[use % 4], 1)
            for i in range(8):
                if i >= 4:
                    pe.wait_ge(bank_free[(QKT_USE + i) % 4], (QKT_USE + i) // 4 + 1)

            def attend(h):
                use = aT_use(h)
                fill(pe, use)
                pe.wait_ge(pa_ready, h + 1)
                for k in range(3):
                    ins = t.transpose(bank(use)[:, P * k:P * k + P], pa[:, P * k:P * k + P], ident[:])
                ins.then_inc(bank_full[use % 4], 1)
                fill(pe, o_use(h))
                pe.wait_ge(bank_free[use % 4], use // 4 + 1)
                vh = v_tok[:, :, VD * h:VD * h + VD]
                use = o_use(h)
                o = bank(use)
                t.matmul(o[:, 0:VD], aT[:, 0:P], vh[:, 0, :], start=True, stop=True)
                t.matmul(o[:, VD:2 * VD], aT[:, P:2 * P], vh[:, 0, :], start=True, stop=False)
                t.matmul(o[:, VD:2 * VD], aT[:, 2 * P:3 * P], vh[:, 1, :], start=False, stop=True).then_inc(
                    bank_full[use % 4], 1)

            pe.wait_ge(bias_step, PARTS)
            for h in range(HEADS):
                par = h % 2
                if h >= 2:
                    pe.wait_ge(exp_done, 4 * (h - 1))
                for part in range(2):
                    sc = PS[4 + 2 * par + part]
                    rows = slice(HD * part, HD * part + HD)
                    t.matmul(sc[:, 0:384], identb[:], maskb[:], start=True, stop=False)
                    t.matmul(sc[:, 0:P], qT[rows, h, 0:P], kT[rows, h, 0:P], start=False, stop=False)
                    ins = t.matmul(sc[:, P:3 * P], qT[rows, h, P:2 * P], kT[rows, h, :], start=False, stop=True)
                ins.then_inc(sc_full, 1)
                if h % 2 == 0:
                    wait_block(GATE0 + h // 2)
                proj(gate_use(h), h1T, h % 2, GATE0 + h // 2, h // 2)
                if h:
                    attend(h - 1)
                if h == MEAN_AT:
                    fill(pe, MEAN_USE)
                    pe.wait_ge(conv_sum, 1)
                    t.matmul(bank(MEAN_USE)[:, 0:T], ones[:], ln_std[:], start=True, stop=True).then_inc(
                        bank_full[MEAN_USE % 4], 1)
                if h == VAR_AT:
                    fill(pe, VAR_USE)
                    pe.wait_ge(conv_sum, 2)
                    t.matmul(bank(VAR_USE)[:, 0:T], ones[:], ln_std[:], start=True, stop=True).then_inc(
                        bank_full[VAR_USE % 4], 1)
            attend(HEADS - 1)

            def conv_out(i):
                if i % 2 == 0:
                    wait_block(COUT0 + i // 2)
                proj(YC_USE[i], conv_acc, i % 2, COUT0 + i // 2, 4 + i // 2)

            pe.wait_ge(swish_ready, KD)
            for i in range(3):
                conv_out(i)
            pe.wait_ge(on_ready, 1)
            for i in range(4):
                use = OT_USE + i
                fill(pe, use)
                for k in range(4):
                    kk = 4 * (i % 2) + k
                    ins = t.transpose(bank(use)[:, P * k:P * k + P], o_tok[:, i // 2, P * kk:P * kk + P], ident[:])
                ins.then_inc(bank_full[use % 4], 1)
            conv_out(3)
            for i in range(4):
                pe.wait_ge(bank_free[(OT_USE + i) % 4], (OT_USE + i) // 4 + 1)
            for i in range(4):
                if i % 2 == 0:
                    wait_block(AOUT0 + i // 2)
                proj(YA_USE + i, oT, i % 2, AOUT0 + i // 2)
            for i in range(4):
                use = MT_USE + i
                pe.wait_ge(mixed, 3 + i // 2)
                fill(pe, use)
                for k in range(4):
                    kk = 4 * (i % 2) + k
                    ins = t.transpose(bank(use)[:, P * k:P * k + P], gates[:, i // 2, P * kk:P * kk + P], ident[:])
                ins.then_inc(bank_full[use % 4], 1)
            wait_block(WO0)
            wait_block(WO0 + 1)
            for i in range(4):
                use = WO_USE + i
                fill(pe, use)
                tt, n = i // 2, WO0 + i % 2
                if n == WO0:
                    for j in (2 * tt, 2 * tt + 1):
                        pe.wait_ge(bank_free[(MT_USE + j) % 4], (MT_USE + j) // 4 + 1)
                for k in range(KD):
                    ins = t.matmul(bank(use)[:, :], mixT[:, k, P * tt:P * tt + P], blk(n)[:, k, :],
                                   start=(k == 0), stop=(k == KD - 1))
                ins.then_inc(bank_full[use % 4], 1)
            pe.wait_ge(in_moe, 16)
            for tt in range(TT):
                pe.wait_ge(x1_ready, 2 * tt + 2)
                for i in range(2):
                    t.matmul(Y[tt][i][:, :], ident[:], x_tok[:, tt, NB * i:NB * i + NB], start=True, stop=True,
                             skip_group_check=True)
                pe.wait_ge(h2_ready, tt + 1)
                for i in (2 * tt, 2 * tt + 1):
                    use = H2T_USE[i]
                    fill(pe, use)
                    for k in range(4):
                        kk = 4 * (i % 2) + k
                        ins = t.transpose(bank(use)[:, P * k:P * k + P], h2[:, tt, P * kk:P * kk + P], ident[:])
                    ins.then_inc(bank_full[use % 4], 1)
                for i in (2 * tt, 2 * tt + 1):
                    pe.wait_ge(bank_free[H2T_USE[i] % 4], H2T_USE[i] // 4 + 1)
                use = LG_USE[tt]
                fill(pe, use)
                for k in range(KD):
                    ins = t.matmul(bank(use)[:, 0:EXPERTS], h2T[:, k, P * tt:P * tt + P], wr[:, k, :],
                                   start=(k == 0), stop=(k == KD - 1))
                ins.then_inc(bank_full[use % 4], 1)
            pe.wait_ge(routed_ready, 1)
            fill(pe, TOT_USE)
            for tt in range(TT):
                ins = t.matmul(bank(TOT_USE)[0:EXPERTS, 0:1], routed[:, tt, :], ones[:, 0:1], start=(tt == 0), stop=(tt == TT - 1))
            ins.then_inc(bank_full[TOT_USE % 4], 1)
            fill(pe, CNT_USE)
            for tt in range(TT):
                ins = t.matmul(bank(CNT_USE)[0:EXPERTS, 0:T], routed[:, tt, :], upper[:, tt, :], start=(tt == 0), stop=(tt == TT - 1))
            ins.then_inc(bank_full[CNT_USE % 4], 1)
            pe.wait_ge(m_ready, 1)
            fill(pe, END_USE)
            e = slice(0, EXPERTS)
            t.matmul(bank(END_USE)[0:3 * EXPERTS, 0:2], tri[:, 0, :, :].rearrange("p a b -> p (a b)"), ecol[e, 1:3],
                     start=True, stop=True)
            t.matmul(bank(END_USE)[0:3 * EXPERTS, 2:3], tri[:, 1, :, :].rearrange("p a b -> p (a b)"), ecol[e, 1:2],
                     start=True, stop=True).then_inc(bank_full[END_USE % 4], 1)
            pe.wait_ge(comb_ready, 1)
            fill(pe, RT_USE)
            for j, src in enumerate((routed, comb)):
                for tt in range(TT):
                    ins = t.transpose(bank(RT_USE)[0:EXPERTS, T * j + P * tt:T * j + P * tt + P], src[:, tt, :], ident[:])
            ins.then_inc(bank_full[RT_USE % 4], 1)
            pe.wait_ge(bank_free[RT_USE % 4], RT_USE // 4 + 1)
            pe.wait_ge(oh_ready, 1)
            fill(pe, UN_USE)
            b = bank(UN_USE)
            for tt in range(TT):
                t.matmul(b[:, P + UCOLS * tt:P + UCOLS * tt + UCOLS], combT[:, P * tt:P * tt + P], onehot[e, :], start=True, stop=True)
            t.matmul(b[:, 0:TT * UCOLS].rearrange("p (t u) -> p t u", t=TT), ones[0:EXPERTS, :],
                     ubase.unsqueeze(1).to_broadcast([EXPERTS, TT, UCOLS]), start=True, stop=False)
            pe.wait_ge(oh_ready, 2)
            for tt in range(TT):
                t.matmul(b[:, UCOLS * tt:UCOLS * tt + UCOLS], rankT[:, P * tt:P * tt + P], onehot[e, :], start=False,
                         stop=(tt == TT - 1))
            for i, (col, rhs) in enumerate(((ecol[e, 7:8], onehot[e, :]), (ones[e, 0:1], l_end), (ecol[e, 8:9], l_one))):
                t.matmul(b[0:1, 256 + UCOLS * i:256 + UCOLS * i + UCOLS], col, rhs, start=True, stop=True)
            for i in range(2):
                ins = t.matmul(b[0:1, 256 + 3 * UCOLS + i:257 + 3 * UCOLS + i], ecol[e, 1 + i:2 + i], ones[e, 0:1],
                               start=True, stop=True)
            ins.then_inc(bank_full[UN_USE % 4], 1)
            pe.wait_ge(units_ready, 2)
            count = pe.value_load(unit_i[0:1, 3 * UCOLS:3 * UCOLS + 1], min_val=TOPK, max_val=47)

            def gather():
                for k in range(KD):
                    for tt in range(TT):
                        for i, part in enumerate(h2_parts):
                            ins = t.matmul(UP[0][:, SLOTS * k:SLOTS * k + SLOTS], part[:, tt, P * k:P * k + P],
                                           pick[:, tt, :], start=(tt == 0 and i == 0), stop=(tt == TT - 1 and i == 2))
                ins.then_inc(gathered, 1)

            def combine(done=None):
                for tt in range(TT):
                    for i in range(2):
                        rows = slice(SLOTS * i, SLOTS * i + SLOTS)
                        ins = t.matmul(Y[tt][i][:, :], Cmb[rows, P * tt:P * tt + P], oe[rows, :], start=False, stop=True,
                                       skip_group_check=True)
                        if done is not None:
                            ins.then_inc(done, 1)

            pe.wait_ge(pick_ready, 1)
            pe.wait_ge(h2_split, 3 * TT)
            gather()
            with pe.Fori(0, count) as u:
                landed = pe.value_load(unit_i[0:1, bass.ds(u, 1)], min_val=16, max_val=16 * EXPERTS)
                spare = pe.value_load(unit_spare[0:1, bass.ds(u, 1)], min_val=0, max_val=16)

                def bias(bank_, col):
                    for i in range(2):
                        t.matmul(bank_[SLOTS * i:SLOTS * i + SLOTS, :], sel, ebias[:, col + NB * i:col + NB * i + NB],
                                 start=True, stop=False)

                def up_chunks(a, chunks, spare_at=0):
                    for k in chunks:
                        slot = 4 * a + k // 2
                        if k % 2 == 0:
                            pe.wait_ge(w_full[slot], landed)
                        for i in range(2):
                            ins = t.matmul(UP[a][SLOTS * i:SLOTS * i + SLOTS, :], xgT[:, k, :],
                                           wslot(slot, spare_at)[:, k % 2, NB * i:NB * i + NB], start=False,
                                           stop=(k == KD - 1))
                        if k % 2 and k < KD - 1:
                            ins.then_inc(w_free, 1)
                    return ins


                def down(a):
                    if a == 0:
                        bias(DOWN, 2 * D)
                    for k in range(4):
                        slot = 8 + 2 * a + k // 2
                        if k % 2 == 0:
                            pe.wait_ge(w_full[slot], landed)
                        for i in range(2):
                            ins = t.matmul(DOWN[SLOTS * i:SLOTS * i + SLOTS, :],
                                           actT[:, a, k % 2, SLOTS * (k // 2):SLOTS * (k // 2) + SLOTS],
                                           wslot(slot)[:, k % 2, NB * i:NB * i + NB],
                                           start=False, stop=(a == 1 and k == 3))
                        if k == 1 or (k == 3 and a == 0):
                            ins.then_inc(w_free, 1)
                    return ins

                def transpose_act(a):
                    for j in range(2):
                        ins = t.transpose(TR[:, T * a + P * j:T * a + P * j + P], act[:, a, P * j:P * j + P], ident[:])
                    ins.then_inc(t_done[a], 1)

                pe.wait_ge(xg_ready, u + 1)
                pe.wait_ge(sel_ready, u + 1)
                bias(UP[0], 0)
                with pe.If(spare == 0):
                    up_chunks(0, range(2 * SPARE))
                with pe.Else():
                    up_chunks(0, range(2 * SPARE), NSLOT * SLOTF)
                up_chunks(0, range(2 * SPARE, KD)).then_inc(up_done[0], 1)
                bias(UP[1], D)
                up_chunks(1, range(KD // 2))
                pe.wait_ge(oe_ready, u + 1)
                pe.wait_ge(cmb_ready, u + 1)
                combine()
                up_chunks(1, range(KD // 2, KD)).then_inc(up_done[1], 1)
                pe.wait_ge(act_ready[0], u + 1)
                transpose_act(0)
                pe.wait_ge(pick_ready, u + 2)
                gather()
                pe.wait_ge(actT_ready[0], u + 1)
                down(0)
                pe.wait_ge(act_ready[1], u + 1)
                transpose_act(1)
                pe.wait_ge(pickw_ready, u + 1)
                pe.wait_ge(actT_ready[1], u + 1)
                for tt in range(TT):
                    ins = t.transpose(TR[:, P * tt:P * tt + P], pickw[:, tt, :], ident[:])
                ins.then_inc(ct_done, 1)
                down(1).then_inc(down_done, 1)
            pe.wait_ge(cmb_ready, count + 1)
            pe.wait_ge(oe_ready, count + 1)
            combine(combined)


_INS = ['x', 'c', 'positions', 'w_ada', 'b_ada', 'norm1_g', 'w_in', 'conv_w', 'conv_b', 'conv_ln_g', 'conv_ln_b',
        'w_conv_out', 'b_conv_out', 'q_norm_g', 'k_norm_g', 'lambda_q1', 'lambda_k1', 'lambda_q2', 'lambda_k2',
        'subln_g', 'w_attn_out', 'b_gate', 'w_o', 'norm2_g', 'w_router', 'b_router', 'w_up', 'b_up', 'w_down', 'b_down']


def kernel(**inputs):
    import numpy as _np
    import concourse.bacc as _bacc
    from concourse.bass_utils import run_bass_kernel_spmd as _run

    nc = _bacc.Bacc("TRN2", target_bir_lowering=False, num_devices=1)
    arrays, args = {}, []
    for name in _INS:
        a = _np.ascontiguousarray(inputs[name])
        arrays[f"in_{name}"] = a
        args.append(nc.dram_tensor(f"in_{name}", a.shape, mybir.dt.from_np(a.dtype), kind="ExternalInput").ap())
    args.append(nc.dram_tensor("out_0", (1, T, D), F32, kind="ExternalOutput").ap())
    build(nc, *args)
    r = _run(nc, [arrays], core_ids=[0])
    return r.results[0]["out_0"]
```
